# Optimizing a Trainium2 kernel written in Bass

```python
import jax, jax.numpy as jnp
from jax import lax
import numpy as np

D_MODEL = 1024
BATCH = 1
SEQ = 1024
DEPTH = 1
DEC_BATCH = 8
DEC_SEQ = 1
PAST_LEN = 1024
PAGE_SIZE = 128

MIX_W = D_MODEL
LRU_W = MIX_W // 2
LRU_BLOCKS = 8
LRU_BW = LRU_W // LRU_BLOCKS
CONV_W = 4
LRU_C = 8.0
N_HEADS = 8
HEAD_DIM = (MIX_W - LRU_W) // N_HEADS
ATT_W = N_HEADS * HEAD_DIM
N_KV_HEADS = 2
KV_GROUP = N_HEADS // N_KV_HEADS
ROT_DIM = HEAD_DIM // 4
ROPE_THETA = 500000.0
IDX_HEADS = 4
IDX_DIM = 64
TOPK_MAX = 256
Q_BLOCK = 128
D_FF = -(-8 * D_MODEL // (3 * 256)) * 256
EPS = 1e-6
IN_SIZES = (LRU_W, LRU_W, ATT_W, N_KV_HEADS * HEAD_DIM, N_KV_HEADS * HEAD_DIM,
            IDX_HEADS * IDX_DIM, IDX_DIM, IDX_HEADS)
IN_W = sum(IN_SIZES)

kernel_name = 'hymba_rglru_dsa_decode_step'

def _split_points():
    pts, acc = [], 0
    for s in IN_SIZES[:-1]:
        acc += s
        pts.append(acc)
    return pts

def rms_norm(x, g):
    xf = x.astype(jnp.float32)
    y = xf * lax.rsqrt(jnp.mean(xf * xf, axis=-1, keepdims=True) + EPS)
    return (y * g.astype(jnp.float32)).astype(x.dtype)

def modulate(h, shift, scale):
    return h * (1.0 + scale[:, None, :]) + shift[:, None, :]

def rope_partial(x, pos):
    half = ROT_DIM // 2
    freq = ROPE_THETA ** (-jnp.arange(half, dtype=jnp.float32) / half)
    ang = pos.astype(jnp.float32)[:, None] * freq
    ang = ang.reshape(ang.shape[:1] + (1,) * (x.ndim - 3) + (half,))
    cos, sin = jnp.cos(ang), jnp.sin(ang)
    xr = x[..., :ROT_DIM].astype(jnp.float32)
    x1, x2 = xr[..., :half], xr[..., half:]
    rot = jnp.concatenate([x1 * cos - x2 * sin, x2 * cos + x1 * sin], axis=-1).astype(x.dtype)
    return jnp.concatenate([rot, x[..., ROT_DIM:]], axis=-1)

def causal_conv(x, buf, w, b):
    t = x.shape[1]
    xp = jnp.concatenate([buf.astype(x.dtype), x], axis=1)
    y = b
    for i in range(CONV_W):
        y = y + xp[:, i:i + t] * w[i]
    return y, xp[:, xp.shape[1] - (CONV_W - 1):]

def rg_lru(x, h0, w_ra, b_ra, w_ix, b_ix, lam):
    bsz, t, c = x.shape
    xb = x.reshape(bsz, t, LRU_BLOCKS, LRU_BW)
    r = jax.nn.sigmoid(jnp.einsum('btni,nij->btnj', xb, w_ra).reshape(bsz, t, c) + b_ra)
    gi = jax.nn.sigmoid(jnp.einsum('btni,nij->btnj', xb, w_ix).reshape(bsz, t, c) + b_ix)
    log_a = -LRU_C * jax.nn.softplus(-lam.astype(jnp.float32)) * r.astype(jnp.float32)
    a = jnp.exp(log_a)
    inp = jnp.sqrt(-jnp.expm1(2.0 * log_a)) * gi.astype(jnp.float32) * x.astype(jnp.float32)

    def combine(left, right):
        a_l, b_l = left
        a_r, b_r = right
        return a_l * a_r, a_r * b_l + b_r

    a_cum, b_cum = lax.associative_scan(combine, (a, inp), axis=1)
    h = a_cum * h0.astype(jnp.float32)[:, None, :] + b_cum
    return h.astype(x.dtype), h[:, -1].astype(h0.dtype)

def sparse_attend(q, iq, iw, q_pos, k_all, v_all, ik_all, k_pos, topk):
    bsz, tq = q.shape[:2]
    s = jnp.einsum('bthd,bsd->bths', iq.astype(jnp.float32), ik_all.astype(jnp.float32)) * IDX_DIM ** -0.5
    score = jnp.einsum('bth,bths->bts', iw.astype(jnp.float32), jax.nn.relu(s)) * IDX_HEADS ** -0.5
    causal = k_pos[None, :] <= q_pos[:, None]
    score = jnp.where(causal[None], score, -jnp.inf)
    _, idx = lax.top_k(score, topk)
    valid = jnp.take(k_pos, idx) <= q_pos[None, :, None]
    bi = jnp.arange(bsz)[:, None, None]
    kg = k_all[bi, idx]
    vg = v_all[bi, idx]
    qg = q.reshape(bsz, tq, N_KV_HEADS, KV_GROUP, HEAD_DIM)
    logits = jnp.einsum('btngd,btsnd->btngs', qg.astype(jnp.float32), kg.astype(jnp.float32)) * HEAD_DIM ** -0.5
    logits = jnp.where(valid[:, :, None, None, :], logits, -jnp.inf)
    p = jax.nn.softmax(logits, axis=-1)
    o = jnp.einsum('btngs,btsnd->btngd', p.astype(vg.dtype), vg)
    return o.reshape(bsz, tq, ATT_W)

def hybrid_layer(x, c, pos, conv_buf, h0, past, lw):
    bsz, t = x.shape[:2]
    mod = jax.nn.silu(c) @ lw['ada_w'] + lw['ada_b']
    sh1, sc1, g1, sh2, sc2, g2 = jnp.split(mod, 6, axis=-1)
    h = modulate(rms_norm(x, lw['ln1_g']), sh1, sc1)
    xr, gr, q, k, v, iq, ik, iw = jnp.split(h @ lw['w_in'], _split_points(), axis=-1)
    xc, conv_new = causal_conv(xr, conv_buf, lw['conv_w'], lw['conv_b'])
    hr, h_last = rg_lru(xc, h0, lw['lru_wa'], lw['lru_ba'], lw['lru_wx'], lw['lru_bx'], lw['lru_lambda'])
    out_a = jax.nn.gelu(gr) * hr
    q = rope_partial(rms_norm(q.reshape(bsz, t, N_HEADS, HEAD_DIM), lw['q_norm_g']), pos)
    k = rope_partial(rms_norm(k.reshape(bsz, t, N_KV_HEADS, HEAD_DIM), lw['k_norm_g']), pos)
    v = v.reshape(bsz, t, N_KV_HEADS, HEAD_DIM)
    iq = rope_partial(iq.reshape(bsz, t, IDX_HEADS, IDX_DIM), pos)
    ik = rope_partial(ik, pos)
    if past is None:
        topk = min(TOPK_MAX, t // 4)
        nblk = t // Q_BLOCK

        def to_blocks(a):
            return jnp.moveaxis(a.reshape((bsz, nblk, Q_BLOCK) + a.shape[2:]), 1, 0)

        def one_block(args):
            qb, iqb, iwb, pb = args
            return sparse_attend(qb, iqb, iwb, pb, k, v, ik, pos, topk)

        ob = lax.map(one_block, (to_blocks(q), to_blocks(iq), to_blocks(iw), pos.reshape(nblk, Q_BLOCK)))
        out_b = jnp.moveaxis(ob, 0, 1).reshape(bsz, t, ATT_W)
    else:
        k_past, v_past, ik_past = past
        n_keys = k_past.shape[1] + t
        topk = min(TOPK_MAX, n_keys // 4)
        k_all = jnp.concatenate([k_past.astype(k.dtype), k], axis=1)
        v_all = jnp.concatenate([v_past.astype(v.dtype), v], axis=1)
        ik_all = jnp.concatenate([ik_past.astype(ik.dtype), ik], axis=1)
        k_pos = jnp.arange(n_keys, dtype=jnp.int32)
        out_b = sparse_attend(q, iq, iw, pos, k_all, v_all, ik_all, k_pos, topk)
    mix = jnp.concatenate([rms_norm(out_a, lw['gn_lru_g']), rms_norm(out_b, lw['gn_att_g'])], axis=-1) @ lw['w_out']
    x = x + g1[:, None, :] * mix
    h2 = modulate(rms_norm(x, lw['ln2_g']), sh2, sc2)
    ff = (jax.nn.silu(h2 @ lw['w_gate']) * (h2 @ lw['w_up'])) @ lw['w_down']
    x = x + g2[:, None, :] * ff
    return x, (k, v, ik, h_last, conv_new)

def setup_inputs(seed: int = 0) -> dict:
    key = jax.random.key(seed)
    ks = jax.random.split(key, 40)
    f32 = jnp.float32

    def nrm(k, shape, scale):
        return jax.random.normal(k, shape, f32) * scale

    def gain(k, shape):
        return 1.0 + 0.01 * jax.random.normal(k, shape, f32)

    n_pages = PAST_LEN // PAGE_SIZE
    n_used = DEC_BATCH * n_pages
    n_pool = n_used + (n_used + 3) // 4
    page_table = jax.random.permutation(ks[0], n_pool)[:n_used].reshape(DEC_BATCH, n_pages).astype(jnp.int32)
    u = jax.random.uniform(ks[1], (DEPTH, LRU_W), f32, 0.9, 0.999)
    base = u ** (1.0 / LRU_C)
    lru_lambda = jnp.log(base) - jnp.log1p(-base)
    return {
        'x_prompt': nrm(ks[2], (BATCH, SEQ, D_MODEL), 1.0),
        'x_sample': nrm(ks[3], (DEC_BATCH, DEC_SEQ, D_MODEL), 1.0),
        'cache_k': nrm(ks[4], (DEPTH, n_pool, PAGE_SIZE, N_KV_HEADS, HEAD_DIM), 1.0),
        'cache_v': nrm(ks[5], (DEPTH, n_pool, PAGE_SIZE, N_KV_HEADS, HEAD_DIM), 1.0),
        'cache_ik': nrm(ks[6], (DEPTH, n_pool, PAGE_SIZE, IDX_DIM), 1.0),
        'state_h': nrm(ks[7], (DEPTH, DEC_BATCH, LRU_W), 0.5),
        'state_conv': nrm(ks[8], (DEPTH, DEC_BATCH, CONV_W - 1, LRU_W), 1.0),
        'page_table': page_table,
        'c_prompt': nrm(ks[9], (BATCH, D_MODEL), 1.0),
        'c_sample': nrm(ks[10], (DEC_BATCH, D_MODEL), 1.0),
        'ada_w': nrm(ks[11], (DEPTH, D_MODEL, 6 * D_MODEL), 0.5 * D_MODEL ** -0.5),
        'ada_b': nrm(ks[12], (DEPTH, 6 * D_MODEL), 0.01),
        'ln1_g': gain(ks[13], (DEPTH, D_MODEL)),
        'w_in': nrm(ks[14], (DEPTH, D_MODEL, IN_W), D_MODEL ** -0.5),
        'conv_w': nrm(ks[15], (DEPTH, CONV_W, LRU_W), CONV_W ** -0.5),
        'conv_b': nrm(ks[16], (DEPTH, LRU_W), 0.01),
        'lru_wa': nrm(ks[17], (DEPTH, LRU_BLOCKS, LRU_BW, LRU_BW), LRU_BW ** -0.5),
        'lru_ba': nrm(ks[18], (DEPTH, LRU_W), 0.01),
        'lru_wx': nrm(ks[19], (DEPTH, LRU_BLOCKS, LRU_BW, LRU_BW), LRU_BW ** -0.5),
        'lru_bx': nrm(ks[20], (DEPTH, LRU_W), 0.01),
        'lru_lambda': lru_lambda,
        'q_norm_g': gain(ks[21], (DEPTH, HEAD_DIM)),
        'k_norm_g': gain(ks[22], (DEPTH, HEAD_DIM)),
        'gn_lru_g': gain(ks[23], (DEPTH, LRU_W)),
        'gn_att_g': gain(ks[24], (DEPTH, ATT_W)),
        'w_out': nrm(ks[25], (DEPTH, MIX_W, D_MODEL), MIX_W ** -0.5),
        'ln2_g': gain(ks[26], (DEPTH, D_MODEL)),
        'w_gate': nrm(ks[27], (DEPTH, D_MODEL, D_FF), D_MODEL ** -0.5),
        'w_up': nrm(ks[28], (DEPTH, D_MODEL, D_FF), D_MODEL ** -0.5),
        'w_down': nrm(ks[29], (DEPTH, D_FF, D_MODEL), D_FF ** -0.5),
    }

def reference(x_prompt, x_sample, cache_k, cache_v, cache_ik, state_h, state_conv, page_table,
              c_prompt, c_sample, ada_w, ada_b, ln1_g, w_in, conv_w, conv_b, lru_wa, lru_ba,
              lru_wx, lru_bx, lru_lambda, q_norm_g, k_norm_g, gn_lru_g, gn_att_g, w_out, ln2_g,
              w_gate, w_up, w_down):
    bsz, t = x_prompt.shape[:2]
    dbsz, dt = x_sample.shape[:2]
    n_pages = page_table.shape[1]
    past_len = n_pages * PAGE_SIZE
    pos_p = jnp.arange(t, dtype=jnp.int32)
    pos_s = past_len + jnp.arange(dt, dtype=jnp.int32)
    yp, ys = x_prompt, x_sample
    st_p, st_s = [], []
    for l in range(DEPTH):
        lw = {'ada_w': ada_w[l], 'ada_b': ada_b[l], 'ln1_g': ln1_g[l], 'w_in': w_in[l],
              'conv_w': conv_w[l], 'conv_b': conv_b[l], 'lru_wa': lru_wa[l], 'lru_ba': lru_ba[l],
              'lru_wx': lru_wx[l], 'lru_bx': lru_bx[l], 'lru_lambda': lru_lambda[l],
              'q_norm_g': q_norm_g[l], 'k_norm_g': k_norm_g[l], 'gn_lru_g': gn_lru_g[l],
              'gn_att_g': gn_att_g[l], 'w_out': w_out[l], 'ln2_g': ln2_g[l],
              'w_gate': w_gate[l], 'w_up': w_up[l], 'w_down': w_down[l]}
        zero_buf = jnp.zeros((bsz, CONV_W - 1, LRU_W), x_prompt.dtype)
        zero_h = jnp.zeros((bsz, LRU_W), state_h.dtype)
        yp, sp = hybrid_layer(yp, c_prompt, pos_p, zero_buf, zero_h, None, lw)
        past = (cache_k[l][page_table].reshape(dbsz, past_len, N_KV_HEADS, HEAD_DIM),
                cache_v[l][page_table].reshape(dbsz, past_len, N_KV_HEADS, HEAD_DIM),
                cache_ik[l][page_table].reshape(dbsz, past_len, IDX_DIM))
        ys, ss = hybrid_layer(ys, c_sample, pos_s, state_conv[l], state_h[l], past, lw)
        st_p.append(sp)
        st_s.append(ss)
    k_prompt = jnp.stack([s[0] for s in st_p])
    v_prompt = jnp.stack([s[1] for s in st_p])
    ik_prompt = jnp.stack([s[2] for s in st_p])
    h_prompt = jnp.stack([s[3] for s in st_p])
    conv_prompt = jnp.stack([s[4] for s in st_p])
    k_sample = jnp.stack([s[0] for s in st_s])
    v_sample = jnp.stack([s[1] for s in st_s])
    ik_sample = jnp.stack([s[2] for s in st_s])
    h_sample = jnp.stack([s[3] for s in st_s])
    conv_sample = jnp.stack([s[4] for s in st_s])
    return (yp, ys, k_prompt, v_prompt, ik_prompt, h_prompt, conv_prompt,
            k_sample, v_sample, ik_sample, h_sample, conv_sample)


_drawn_inputs = setup_inputs


def setup_inputs(seed=0):
    import zlib

    import numpy as np

    out = dict(_drawn_inputs(seed))
    spreads = {}
    factors = {'lru_ba': 28.348,
     'lru_bx': 8.0,
     'q_norm_g': 8.0,
     'k_norm_g': 7.06,
     'gn_lru_g': 45.143,
     'gn_att_g': 47.725,
     'ln2_g': 31.167}
    for name, (base, spread) in spreads.items():
        noise = np.random.default_rng([zlib.crc32(name.encode()), seed]).standard_normal(out[name].shape)
        drawn = base * np.exp(spread * noise) if base else spread * noise
        out[name] = __import__('jax').numpy.asarray(drawn.astype(out[name].dtype))
    for name, factor in factors.items():
        out[name] = (out[name] * factor).astype(out[name].dtype)
    return out
```

```python
from contextlib import ExitStack

import numpy as np

import concourse.bass as bass
from concourse import mybir

P = 128
ALU = mybir.AluOpType
ACT = mybir.ActivationFunctionType
AX = mybir.AxisListType
F32 = mybir.dt.float32
F32R = mybir.dt.float32r
BF16 = mybir.dt.bfloat16
I32 = mybir.dt.int32

D = 1024
KD = D // P
T = 1024
NB = 8
NTOK = T + NB
NCH = 3
CW = NTOK // NCH
TAIL = CW - NB
NTT = T // P
ALLT = NTT + 1
LRU = 512
LT = LRU // P
NH, NKV, HD = 8, 2, 64
GRP = NH // NKV
IH = 4
TOPK = 256
QK = NH * HD + NKV * HD
IQK = IH * HD + HD + IH
HALF = 8
PG = 8
NPOOL = 80
NKEY = PG * P + 1
DFF = 2816
FT = DFF // P
EPS = 1e-6
C_LRU = 8.0
SCALE = HD ** -0.5
NEG = -1.0e30
FIRST_SEL = TOPK // P

C_ID, C_CAUS, C_ONE, C_E4, C_E4T, C_M4, C_E8, C_E8T, C_ROPE = 0, 128, 256, 384, 416, 424, 428, 492, 500
C_ALL = C_ROPE + ALLT * 2 * HALF

V_LN1, V_LN2, V_CW, V_CB, V_BA, V_BX, V_LAM, V_GL, V_GA, V_ADA = 0, 8, 16, 32, 36, 40, 44, 48, 52, 56
V_ALL = 104

CHUNKS = [(1792, IQK), (1024, 384), (1408, 384)]

NU_LRU, NU_OUT = 8, 8
U_OUT = NU_LRU
U_FFN = NU_LRU + NU_OUT
FB = FT // 2
UPB = 6
SLOTS = 3

S_OFF = {}
_o = 0
for _i in range(FIRST_SEL, NTT):
    S_OFF[_i] = _o
    _o += P * (_i + 1)
S_DEC = _o
S_ALL = _o + NKEY
SEL = [(i, P, P * (i + 1), S_OFF[i]) for i in range(FIRST_SEL, NTT)] + [(NTT, NB, NKEY, S_DEC)]
NSEL = len(SEL)


def halves(w):
    return [(a, min(512, w - a)) for a in range(0, w, 512)]


def build(nc, a, o):
    ctx = ExitStack()
    with ctx:
        def sb(name, shape, dt=F32):
            return ctx.enter_context(nc.sbuf_tensor(name, shape, dt))

        def sem(name):
            return ctx.enter_context(nc.semaphore(name))

        consts = sb("consts", [P, C_ALL])
        ident = consts[:, C_ID:C_ID + P]
        caus = consts[:, C_CAUS:C_CAUS + P]
        ones = consts[:, C_ONE:C_ONE + P]
        vec = sb("vec", [P, V_ALL])
        stT = sb("stT", [P, P])
        gqk = sb("gqk", [P, 2, HD])
        mod = sb("mod", [P, 48, 1 + NB])
        g1p = sb("g1p", [P, KD, 1 + NB])
        wbd = sb("wbd", [P, 2, LT, P])
        nsp = sb("nsp", [P, 4, LT])
        sp2 = sb("sp2", [P, 3, LT])
        pt_sb = sb("pt_sb", [1, NB * PG], I32)
        lasts = sb("lasts", [P, 80])
        keyK = sb("keyK", [P, NSEL], I32)
        keyC = sb("keyC", [P, NSEL], I32)
        keyX = sb("keyX", [P, NSEL], I32)
        keyM = sb("keyM", [P, NSEL], I32)
        keep = sb("keep", [P, NSEL], I32)
        bit = sb("bit", [P, 1], I32)
        cnt = sb("cnt", [P, NSEL])
        rstd = sb("rstd", [P, ALLT, NH + NKV])
        mx = sb("mx", [P, 2])
        nb = sb("nb", [P, 2])
        rsum = sb("rsum", [P, NH])
        rinv = sb("rinv", [P, NH])
        dsm = sb("dsm", [64, 8])
        iwc = sb("iwc", [32, 8])
        iwb = sb("iwb", [32, NB])
        samp = sb("samp", [P, KD, NB])
        samp2 = sb("samp2", [P, KD, NB])

        base = nc.sbuf_base
        RH, RP = base, base + 2 * KD * NTOK * 4
        size = 2 * KD * NTOK * 4 + 133504
        ctx.enter_context(nc.sbuf_tensor("arena", [P, size // 4], F32))

        def at(name, shape, off, dt=F32):
            return nc.alloc_sbuf_tensor_at(name, shape, dt, offset=off)

        A_X = RP + 100480
        hH = at("hH", [P, KD, NTOK], RH, F32R)
        hL = at("hL", [P, KD, NTOK], RH + KD * NTOK * 4, F32R)
        xin = at("xin", [P, NTT, D], RH)
        xT = at("xT", [P, KD, NTOK], A_X)
        ada = [at(f"ada{i}", [P, KD, 512], RP + 16384 * i) for i in range(4)]
        sq = [at(f"sq{i}", [P, NTOK], RP + 65600 + 4160 * i) for i in range(2)]
        rb = at("rb", [P, NTOK], RP + 73920)
        tt = at("tt", [P, NTOK], RP + 78080)
        xs_in = at("xs_in", [NB, D], RP + 82240)
        c_in = at("c_in", [1 + NB, D], RP + 86336)
        c_si = at("c_si", [1 + NB, D], RP + 90432)
        cT = at("cT", [P, KD, 1 + NB], RP + 94528)
        vrows = at("vrows", [V_ALL, P], RP + 94848)
        strows = at("strows", [P, P], RP + 95360)
        grow = at("grow", [1, P], RP + 95872)
        qk = at("qk", [P, ALLT, QK], RP)
        vt = at("vt", [P, ALLT, P], RP + 23040)
        iqk = at("iqk", [P, ALLT, IQK], RP + 27648)
        craw = [at("craw0", [P, KD, 384], RP + 83200), at("craw1", [P, KD, 384], RP + 39328)]
        cH = [at("cH0", [P, KD, 384], RP + 51616, F32R), at("cH1", [P, KD, 384], RP + 95488, F32R)]
        cL = [at("cL0", [P, KD, 384], RP + 63904, F32R), at("cL1", [P, KD, 384], RP + 107776, F32R)]
        score = at("score", [P, S_ALL], RP + 39328)
        RING = RP + 60352
        wraw = [at(f"wraw{i}", [P, KD, P], RING + 4096 * i) for i in range(SLOTS)]
        wH = [at(f"wH{i}", [P, KD, P], RING + 12288 + 8192 * i, F32R) for i in range(SLOTS)]
        wL = [at(f"wL{i}", [P, KD, P], RING + 12288 + 8192 * i + 4096, F32R) for i in range(SLOTS)]
        Q5 = RING + 36864
        ikT = at("ikT", [P, 2, T], Q5, F32R)
        istk = [at(f"istk{i}", [P, IH, 2, HD], Q5 + 8192 + 3072 * i) for i in range(2)]
        ikstk = [at(f"ikstk{i}", [P, 2, 2, HD], Q5 + 10240 + 3072 * i) for i in range(2)]
        iqT = [at(f"iqT{i}", [P, IH, P], Q5 + 14336 + 2048 * i, F32R) for i in range(2)]
        relu = [at(f"relu{i}", [P, T], Q5 + 18432 + 4096 * i) for i in range(2)]
        rt5 = at("rt5", [P, 4, ALLT * (NH + NKV) * HALF], RING)
        ipg = [at(f"ipg{i}", [P, PG, HD], RING + 12288 + 2048 * i) for i in range(2)]
        ikb = [at(f"ikb{i}", [HD, NKEY], RING + 16384 + 4160 * i) for i in range(2)]
        iqb = at("iqb", [HD, NB, 36], RING + 24704)
        iknew = at("iknew", [HD, NB], RING + 25856)
        reld = at("reld", [32, NKEY], RING + 25920)
        qsq = at("qsq", [P, ALLT, QK], Q5 + 8192)
        junk = at("junk", [P, S_ALL], RP + 27648, BF16)
        eqb = at("eqb", [P, NKEY], RP + 29760)
        preb = at("preb", [P, NKEY], RP + 33920)
        xr = at("xr", [P, LT, NTOK + 3], Q5)
        gel = at("gel", [P, LT, NTOK], Q5 + 16576)
        kT = at("kT", [P, NKV, 2, T], RH, F32R)
        stk = at("stk", [P, NH, 2, HD], RH + 16384)
        qT = at("qT", [P, NH, P], RH + 20480, F32R)
        lg = [at(f"lg{i}", [P, T], RH + 24576 + 4096 * i) for i in range(2)]
        pT = [at(f"pT{i}", [P, NTT, P], RH + 32768 + 4096 * i) for i in range(2)]
        ob = at("ob", [P, NH * HD], RH + 40960)
        lru_t = [at(f"lru{i}", [P, NTOK], RH + 43008 + 4160 * i) for i in range(4)]
        lrow = at("lrow", [80, P], RH + 59712)
        attT = at("attT", [P, ALLT, LT, P], RP)
        kpg = [at(f"kpg{i}", [P, PG, P], RH + 4096 * i) for i in range(2)]
        vpg = [at(f"vpg{i}", [P, PG, P], RH + 8192 + 4096 * i) for i in range(2)]
        kbT = [at(f"kbT{i}", [P, NKEY], RH + 16384 + 4160 * i) for i in range(2)]
        qb = at("qb", [P, NB, 72], RH + 24704)
        knew = at("knew", [P, NB], RH + 27008)
        dlg = at("dlg", [64, NKEY], RH + 27072)
        dpT = at("dpT", [P, PG, 64], RH + 31232)
        ddg = at("ddg", [64, 64], RH + 33280)
        ptl = at("ptl", [NB, 64], RH + 33536)
        nsq = [at(f"nsq{i}", [P, NTOK], RP + 39328 + 4160 * i) for i in range(2)]
        nr = [at(f"nr{i}", [P, NTOK], RP + 47648 + 4160 * i) for i in range(2)]
        nt = at("nt", [P, NTOK], RP + 55968)
        mixH = at("mixH", [P, KD, NTOK], RH, F32R)
        mixL = at("mixL", [P, KD, NTOK], RH + KD * NTOK * 4, F32R)
        h2H = at("h2H", [P, KD, NTOK], RH, F32R)
        h2L = at("h2L", [P, KD, NTOK], RH + KD * NTOK * 4, F32R)
        aH = at("aH", [P, 2, NTOK], RP, F32R)
        aL = at("aL", [P, 2, NTOK], RP + 8256, F32R)
        sg = at("sg", [P, NTOK], RP + 16512)
        af = at("af", [P, NTOK], RP + 20672)
        yo = [at(f"yo{i}", [P, D], RP + 39328 + 4096 * i) for i in range(2)]

        ps = ctx.enter_context(nc.psum_tensor("ps", [P, 8, 512], F32))
        spill = nc.dram_tensor("x_feature_major", (P, KD, NTOK), F32).ap()

        def wide(b):
            return ps[:, b:b + 3, 0:CW]

        def cols(ap):
            return ap.rearrange("p (c n) -> p c n", c=NCH)

        s_const = sem("const_loaded")
        s_small = sem("small_loaded")
        s_wbd0 = sem("gate_weights_cleared")
        s_wbd = sem("gate_weights_loaded")
        s_x = [sem(f"x_loaded{i}") for i in range(NTT)]
        s_ada = [sem(f"ada_loaded{i}") for i in range(4)]
        s_modk = sem("ada_chunk_used")
        s_csi = sem("c_silu_done")
        s_tr = sem("x_transposed")
        s_xta = sem("x_evacuated_act")
        s_xtv = sem("x_evacuated_dve")
        s_mt = sem("small_transposed")
        s_mte = sem("small_evacuated")
        s_exl = sem("exp_lambda")
        s_ikst = sem("index_keys_stored")
        s_kvst = sem("keys_values_stored")
        s_sq = sem("squares_ready")
        s_squ = sem("squares_used")
        s_var = sem("variance_ready")
        s_rt = sem("root_ready")
        s_t = sem("norm_ready")
        s_h = sem("high_ready")
        s_l = sem("low_ready")
        s_spill = sem("x_spilled")
        s_craw = [sem(f"chunk_loaded{i}") for i in range(2)]
        s_cH = sem("chunk_high")
        s_cL = sem("chunk_low")
        s_pj = sem("proj_done")
        s_pja = sem("proj_evacuated_act")
        s_pjv = sem("proj_evacuated_dve")
        s_clr = sem("sample_rows_cleared")
        s_qsq = sem("qk_squares")
        s_qv = sem("qk_variance")
        s_qr = sem("qk_root")
        s_qkr = sem("qk_rotated")
        s_iqr = sem("iq_rotated")
        s_is = sem("index_high")
        s_il = sem("index_low")
        s_it = sem("index_transposed")
        s_ite = sem("index_transposed_evacuated")
        s_ikte = sem("index_keys_evacuated")
        s_sc = sem("scores_product")
        s_re = sem("scores_relu")
        s_sa = sem("scores_added")
        s_ipg = [sem(f"index_page_loaded{i}") for i in range(2)]
        s_dit = sem("decode_index_transposed")
        s_die = sem("decode_index_evacuated")
        s_dis = sem("decode_index_product")
        s_dir = sem("decode_index_relu")
        s_diw = sem("decode_iw")
        s_dsc = sem("decode_scores")
        s_sel = sem("selection_done")
        s_wr = [sem(f"unit_loaded{i}") for i in range(SLOTS)]
        s_wH = sem("unit_high")
        s_wL = sem("unit_low")
        s_un = sem("unit_used")
        s_lev = sem("lru_evacuated")
        s_xc = sem("conv_done")
        s_gp = sem("gate_product")
        s_gs = sem("gate_sigmoid")
        s_ga = sem("decay_ready")
        s_lu = sem("lru_root_input")
        s_lq = sem("lru_root")
        s_lh = sem("lru_tile_done")
        s_lt = sem("lasts_transposed")
        s_lte = sem("lasts_evacuated")
        s_kst = sem("k_stack")
        s_kt = sem("k_transposed")
        s_kte = sem("k_evacuated")
        s_qs = sem("q_stack_high")
        s_ql = sem("q_stack_low")
        s_qt = sem("q_transposed")
        s_qte = sem("q_evacuated")
        s_lg = sem("logits_ready")
        s_lm = sem("logits_masked")
        s_ex = sem("probs_ready")
        s_ptt = sem("probs_transposed")
        s_pte = sem("probs_evacuated")
        s_pv = sem("values_mixed")
        s_ob = sem("heads_normalised")
        s_ot = sem("heads_transposed")
        s_ote = sem("heads_evacuated")
        s_kpg = [sem(f"k_pages_loaded{i}") for i in range(2)]
        s_vpg = [sem(f"v_pages_loaded{i}") for i in range(2)]
        s_dqt = sem("decode_q_transposed")
        s_dqe = sem("decode_q_evacuated")
        s_dkt = sem("decode_keys_transposed")
        s_dke = sem("decode_keys_evacuated")
        s_dlg = sem("decode_logits")
        s_dmx = sem("decode_max")
        s_dex = sem("decode_exp")
        s_dpn = sem("decode_probs")
        s_dpt = sem("decode_probs_transposed")
        s_dpe = sem("decode_probs_evacuated")
        s_dpu = sem("decode_pages_used")
        s_dat = sem("decode_heads_placed")
        s_gsq = sem("group_squares")
        s_gsu = sem("group_squares_used")
        s_gv = sem("group_variance")
        s_gr = sem("group_root")
        s_gt = sem("group_norm")
        s_gH = sem("mix_high")
        s_gL = sem("mix_low")
        s_xback = sem("x_reloaded")
        s_res = sem("residual_added")
        s_a2 = sem("second_mod_ready")
        s_sq2 = sem("squares2_ready")
        s_su2 = sem("squares2_used")
        s_v2 = sem("variance2_ready")
        s_r2 = sem("root2_ready")
        s_t2 = sem("norm2_ready")
        s_h2 = sem("high2_ready")
        s_l2 = sem("low2_ready")
        s_sg = sem("gate_silu")
        s_af = sem("ffn_product")
        s_aH = sem("ffn_high")
        s_aL = sem("ffn_low")
        s_dn = sem("down_product")
        s_dne = sem("down_added")
        s_yt = sem("y_transposed")
        s_yea = sem("y_evacuated")
        s_y = sem("y_final")
        s_yst = [sem(f"y_stored{i}") for i in range(2)]
        s_out = sem("outputs_stored")
        s_outs = sem("outputs_stored_pool")

        w_in = a["w_in"][0]
        gate_src = a["w_gate"][0].rearrange("(k p) n -> p k n", p=P)
        up_src = a["w_up"][0].rearrange("(k p) n -> p k n", p=P)
        out_src = a["w_out"][0].rearrange("(k p) n -> p k n", p=P)
        in_src = w_in.rearrange("(k p) n -> p k n", p=P)
        ada_src = a["ada_w"][0].rearrange("(k p) n -> p k n", p=P)
        N_OUT = [0]

        block = ctx.enter_context(nc.Block())

        @block.sync
        def _(sp):
            sp.dma_start(consts[:], a["consts"]).then_inc(s_const, 16)
            sp.dma_start(c_in[0:1, :], a["c_prompt"]).then_inc(s_small, 16)
            sp.dma_start(c_in[1:1 + NB, :], a["c_sample"]).then_inc(s_small, 16)
            sp.dma_start(xs_in[:], a["x_sample"].rearrange("b t d -> (b t) d")).then_inc(s_small, 16)
            for name, row, n in (("ln1_g", V_LN1, 8), ("ln2_g", V_LN2, 8), ("conv_b", V_CB, 4), ("lru_ba", V_BA, 4),
                                 ("lru_bx", V_BX, 4), ("lru_lambda", V_LAM, 4), ("gn_lru_g", V_GL, 4),
                                 ("gn_att_g", V_GA, 4), ("ada_b", V_ADA, 48)):
                sp.dma_start(vrows[row:row + n, :], a[name][0].rearrange("(r f) -> r f", f=P)).then_inc(s_small, 16)
            sp.dma_start(vrows[V_CW:V_CW + 16, :],
                         a["conv_w"][0].rearrange("i (c f) -> (i c) f", f=P)).then_inc(s_small, 16)
            sp.dma_start(strows[0:32, :], a["state_h"][0].rearrange("b (c f) -> (b c) f", f=P)).then_inc(s_small, 16)
            sp.dma_start(strows[32:128, :],
                         a["state_conv"][0].rearrange("b i (c f) -> (b i c) f", f=P)).then_inc(s_small, 16)
            sp.dma_start(grow[0:1, 0:HD], a["q_norm_g"]).then_inc(s_small, 16)
            sp.dma_start(grow[0:1, HD:2 * HD], a["k_norm_g"]).then_inc(s_small, 16)
            sp.dma_start(pt_sb[:], a["page_table"].rearrange("(a b) g -> a (b g)", a=1)).then_inc(s_small, 16)
            for i in range(NTT):
                sp.dma_start(xin[:, i, :], a["x_prompt"][0, i * P:(i + 1) * P, :]).then_inc(s_x[i], 16)
            for j in range(12):
                if j >= 4:
                    sp.wait_ge(s_modk, j - 3)
                sp.dma_start(ada[j % 4][:], ada_src[:, :, j * 512:(j + 1) * 512]).then_inc(s_ada[j % 4], 16)
            sp.wait_ge(s_l, KD + 1)
            sp.dma_start(spill, xT[:]).then_inc(s_spill, 16)
            for j, (c0, w) in enumerate(CHUNKS):
                if j == 0:
                    sp.wait_ge(s_modk, 12)
                    sp.wait_ge(s_mte, 3)
                if j == 2:
                    sp.wait_ge(s_cL, 1)
                sp.dma_start(craw[j % 2][:, :, 0:w], in_src[:, :, c0:c0 + w]).then_inc(s_craw[j % 2], 16)
            sp.wait_ge(s_pj, 27)
            for b in range(NB):
                if b >= 2:
                    sp.wait_ge(s_dit, b - 1)
                for g in range(PG):
                    page = sp.value_load(pt_sb[0:1, b * PG + g:b * PG + g + 1], min_val=0, max_val=NPOOL - 1)
                    sp.dma_start(ipg[b % 2][:, g, :],
                                 a["cache_ik"][0][bass.ds(page, 1), :, :].rearrange("a s d -> (a s) d")
                                 ).then_inc(s_ipg[b % 2], 16)
            sp.wait_ge(s_iqr, 1)
            sp.dma_start(o["ik_prompt"][0, 0].rearrange("(t p) d -> p t d", p=P),
                         iqk[:, 0:NTT, IH * HD:IH * HD + HD]).then_inc(s_ikst, 16)
            sp.dma_start(o["ik_sample"][0].rearrange("b t d -> (b t) d"),
                         iqk[0:NB, NTT, IH * HD:IH * HD + HD]).then_inc(s_ikst, 16)
            sp.wait_ge(s_pja, 19)
            sp.wait_ge(s_pjv, 13)
            sp.dma_start(o["v_prompt"][0, 0].rearrange("(t p) k d -> p t (k d)", p=P),
                         vt[:, 0:NTT, :]).then_inc(s_kvst, 16)
            sp.dma_start(o["v_sample"][0].rearrange("b t k d -> (b t) (k d)"), vt[0:NB, NTT, :]).then_inc(s_kvst, 16)
            sp.wait_ge(s_qkr, 1)
            sp.dma_start(o["k_prompt"][0, 0].rearrange("(t p) k d -> p t (k d)", p=P),
                         qk[:, 0:NTT, NH * HD:QK]).then_inc(s_kvst, 16)
            sp.dma_start(o["k_sample"][0].rearrange("b t k d -> (b t) (k d)"),
                         qk[0:NB, NTT, NH * HD:QK]).then_inc(s_kvst, 16)
            sp.dma_start(o["conv_sample"][0, :, 0:2, :], a["state_conv"][0, :, 1:3, :]).then_inc(s_out, 16)

            def load_unit(u, src, first=False):
                if u >= SLOTS:
                    sp.wait_ge(s_wL, u - SLOTS + 1)
                sp.dma_start(wraw[u % SLOTS][:], src).then_inc(s_wr[u % SLOTS], 16)

            sp.wait_ge(s_dsc, 1)
            sp.wait_ge(s_qkr, 1)
            for u in range(NU_LRU):
                c0 = (u // 2) * P + (u % 2) * LRU
                load_unit(u, in_src[:, :, c0:c0 + P])
            for n in range(6):
                load_unit(U_OUT + n, out_src[:, :, n * P:(n + 1) * P])
            sp.wait_ge(s_lte, 1)
            sp.dma_start(o["h_prompt"][0, 0].rearrange("(c f) -> c f", f=P), lrow[0:4, :]).then_inc(s_out, 16)
            sp.dma_start(o["h_sample"][0].rearrange("b (c f) -> (b c) f", f=P), lrow[4:36, :]).then_inc(s_out, 16)
            sp.dma_start(o["conv_prompt"][0, 0].rearrange("i (c f) -> (i c) f", f=P),
                         lrow[36:48, :]).then_inc(s_out, 16)
            sp.dma_start(o["conv_sample"][0, :, 2, :].rearrange("b (c f) -> b c f", f=P),
                         lrow[48:80, :]).then_inc(s_out, 16)
            sp.wait_ge(s_ote, NTT)
            for b in range(NB):
                if b >= 2:
                    sp.wait_ge(s_dkt, b - 1)
                for g in range(PG):
                    page = sp.value_load(pt_sb[0:1, b * PG + g:b * PG + g + 1], min_val=0, max_val=NPOOL - 1)
                    sp.dma_start(kpg[b % 2][:, g, :],
                                 a["cache_k"][0][bass.ds(page, 1)].rearrange("a s k d -> (a s) (k d)")
                                 ).then_inc(s_kpg[b % 2], 16)
            for b in range(NB):
                if b >= 2:
                    sp.wait_ge(s_dpu, b - 1)
                for g in range(PG):
                    page = sp.value_load(pt_sb[0:1, b * PG + g:b * PG + g + 1], min_val=0, max_val=NPOOL - 1)
                    sp.dma_start(vpg[b % 2][:, g, :],
                                 a["cache_v"][0][bass.ds(page, 1)].rearrange("a s k d -> (a s) (k d)")
                                 ).then_inc(s_vpg[b % 2], 16)
            for n in range(6, NU_OUT):
                load_unit(U_OUT + n, out_src[:, :, n * P:(n + 1) * P])
            sp.wait_ge(s_gL, 8)
            sp.wait_ge(s_spill, 16)
            sp.dma_start(xT[:], spill).then_inc(s_xback, 16)

            with sp.Fori(0, FB) as i:
                for k in range(UPB):
                    u = U_FFN + k
                    sp.wait_ge(s_wL, i * UPB + (u - SLOTS + 1))
                    if k < 4:
                        m = (gate_src, up_src)[k % 2]
                        src = m[:, :, bass.ds(i * (2 * P) + (k // 2) * P, P)]
                        sp.dma_start(wraw[u % SLOTS][:], src).then_inc(s_wr[u % SLOTS], 16)
                    else:
                        src = a["w_down"][0][bass.ds(i * (2 * P) + (k - 4) * P, P), :]
                        sp.dma_start(wraw[u % SLOTS][:].rearrange("p k n -> p (k n)"), src
                                     ).then_inc(s_wr[u % SLOTS], 16)
            for i in range(ALLT):
                sp.wait_ge(s_yea, 2 * i + 2)
                if i < NTT:
                    sp.dma_start(o["y_prompt"][0, i * P:(i + 1) * P, :], yo[i % 2][:]).then_inc(s_yst[i % 2], 16)
                else:
                    sp.dma_start(o["y_sample"].rearrange("b t d -> (b t) d"),
                                 yo[i % 2][0:NB, :]).then_inc(s_yst[i % 2], 16)
            sp.wait_ge(s_yst[0], 16 * 5)
            sp.wait_ge(s_yst[1], 16 * 4)
            sp.wait_ge(s_ikst, 16 * 2)
            sp.wait_ge(s_kvst, 16 * 4)
            sp.wait_ge(s_out, 16 * 5)

        @block.gpsimd
        def _(pool):
            pool.memset(wbd[:], 0.0).then_inc(s_wbd0, 1)
            pool.wait_ge(s_wbd0, 1)
            for gate, name in enumerate(("lru_wa", "lru_wx")):
                for h in range(2):
                    pool.dma_start(wbd[h * 64:(h + 1) * 64, gate, :, h * 64:(h + 1) * 64],
                                   a[name][0].rearrange("(c h) i j -> h i c j", h=2)[h]).then_inc(s_wbd, 16)
            for j, (c0, w) in enumerate(CHUNKS):
                pool.wait_ge(s_cH, j + 1)
                if j == 1:
                    pool.wait_ge(s_spill, 16)
                if j == 2:
                    pool.wait_ge(s_pj, 9)
                pool.tensor_tensor(cL[j % 2][:, :, 0:w], craw[j % 2][:, :, 0:w],
                                   cH[j % 2][:, :, 0:w].bitcast(F32), ALU.subtract).then_inc(s_cL, 1)

            for u in range(U_FFN):
                s = u % SLOTS
                pool.wait_ge(s_wH, u + 1)
                pool.tensor_tensor(wL[s][:], wraw[s][:], wH[s][:].bitcast(F32), ALU.subtract).then_inc(s_wL, 1)
            with pool.Fori(0, FB) as i:
                for k in range(UPB):
                    s = (U_FFN + k) % SLOTS
                    pool.wait_ge(s_wH, i * UPB + (U_FFN + k + 1))
                    pool.tensor_tensor(wL[s][:], wraw[s][:], wH[s][:].bitcast(F32), ALU.subtract).then_inc(s_wL, 1)

        @block.scalar
        def _(act):
            A = nc.scalar.activation

            act.wait_ge(s_small, 16 * 18)
            A(c_si[:], c_in[:], ACT.Silu).then_inc(s_csi, 1)
            for g in range(0, 16, 2):
                act.wait_ge(s_tr, g + 1)
                i, hf = g // 2, g % 2
                nc.scalar.copy(xT[:, 4 * hf:4 * hf + 4, i * P:(i + 1) * P],
                               ps[:, g % 4, :].rearrange("p (k t) -> p k t", k=4)).then_inc(s_xta, 1)
            act.drain()
            act.wait_ge(s_xtv, 8)
            act.wait_ge(s_mte, 3)
            A(sp2[:, 0, :], sp2[:, 0, :], ACT.Exp, scale=-1.0).then_inc(s_exl, 1)
            for d in range(KD):
                if d >= 2:
                    act.wait_ge(s_squ, d - 1)
                A(sq[d % 2][:], xT[:, d, :], ACT.Square).then_inc(s_sq, 1)
            act.wait_ge(s_var, 1)
            A(rb[:], rb[:], ACT.Sqrt).then_inc(s_rt, 1)
            for d in range(KD):
                act.wait_ge(s_t, d + 1)
                A(hH[:, d, 0:T], tt[:, 0:T], ACT.Identity, bias=mod[:, d, 0:1]).then_inc(s_h, 1)
            act.wait_ge(s_t, KD + 1)
            nc.scalar.copy(hH[:, :, T:NTOK], samp[:]).then_inc(s_h, 1)

            def chunk_high(j):
                w = CHUNKS[j][1]
                act.wait_ge(s_craw[j % 2], 16 * (j // 2 + 1))
                if j == 0:
                    act.wait_ge(s_l, KD + 1)
                if j == 1:
                    act.wait_ge(s_spill, 16)
                if j == 2:
                    act.wait_ge(s_pj, 9)
                nc.scalar.copy(cH[j % 2][:, :, 0:w], craw[j % 2][:, :, 0:w]).then_inc(s_cH, 1)

            chunk_high(0)
            chunk_high(1)
            for n in range(0, 27, 2):
                j, i = n // 9, n % 9
                m = P if i < NTT else NB
                if n == 10:
                    chunk_high(2)
                if n == 0:
                    act.wait_ge(s_clr, 1)
                act.wait_ge(s_pj, n + 1)
                if j == 0:
                    nc.scalar.copy(iqk[0:m, i, :], ps[0:m, n % 6, 0:IQK]).then_inc(s_pja, 1)
                elif j == 1:
                    nc.scalar.copy(qk[0:m, i, 0:384], ps[0:m, n % 6, 0:384]).then_inc(s_pja, 1)
                else:
                    nc.scalar.copy(qk[0:m, i, 384:QK], ps[0:m, n % 6, 0:256]).then_inc(s_pja, 1)
                    nc.scalar.copy(vt[0:m, i, :], ps[0:m, n % 6, 256:384]).then_inc(s_pja, 1)
            act.drain()
            act.wait_ge(s_iqr, 1)
            for i in range(NTT):
                s = i % 2
                if i >= 2:
                    act.wait_ge(s_it, i - 1)
                nc.scalar.copy(istk[s][:, :, 0, :].bitcast(F32R),
                               iqk[:, i, 0:IH * HD].rearrange("p (h d) -> p h d", h=IH)).then_inc(s_is, 1)
                for r in range(2):
                    nc.scalar.copy(ikstk[s][:, 0, r, :].bitcast(F32R),
                                   iqk[:, i, IH * HD:IH * HD + HD]).then_inc(s_is, 1)
                act.wait_ge(s_it, i + 1)
                if i >= 2:
                    act.wait_ge(s_sc, IH * max(0, i - 1 - FIRST_SEL)) if i - 1 > FIRST_SEL else None
                nc.scalar.copy(iqT[s][:], ps[:, 4 + s, :].rearrange("p (h t) -> p h t", h=IH)).then_inc(s_ite, 1)
                nc.scalar.copy(ikT[:, :, i * P:(i + 1) * P],
                               ps[:, 6 + s, 0:256].rearrange("p (r t) -> p r t", r=2)).then_inc(s_ikte, 1)
                if i >= FIRST_SEL:
                    w = P * (i + 1)
                    for h in range(IH):
                        g = IH * (i - FIRST_SEL) + h
                        act.wait_ge(s_sc, g + 1)
                        if g >= 2:
                            act.wait_ge(s_sa, g - 1)
                        A(relu[g % 2][:, 0:w],
                          ps[:, 2 * (g % 2):2 * (g % 2) + 2, :].rearrange("p b n -> p (b n)")[:, 0:w],
                          ACT.Relu).then_inc(s_re, 1)
            act.wait_ge(s_dis, 1)
            A(reld[:, 0:1024], ps[0:32, 0:2, :].rearrange("p b n -> p (b n)"), ACT.Relu).then_inc(s_dir, 1)
            A(reld[:, 1024:1025], ps[0:32, 2, 0:1], ACT.Relu).then_inc(s_dir, 1)
            act.wait_ge(s_sa, IH * (NTT - FIRST_SEL))
            act.wait_ge(s_ikte, NTT)
            act.drain()
            A(qsq[:], qk[:], ACT.Square).then_inc(s_qsq, 1)
            act.wait_ge(s_qv, 1)
            A(rstd[:], rstd[:], ACT.Sqrt).then_inc(s_qr, 1)

            def high(u):
                s = u % SLOTS
                act.wait_ge(s_wr[s], 16 * (u // SLOTS + 1))
                if u >= SLOTS:
                    act.wait_ge(s_un, u - SLOTS + 1)
                nc.scalar.copy(wH[s][:], wraw[s][:]).then_inc(s_wH, 1)

            high(0)
            act.wait_ge(s_qkr, 1)
            for u in range(NU_LRU):
                c = u // 2
                high(u + 1)
                act.wait_ge(s_un, u + 1)
                if u % 2 == 0:
                    nc.scalar.copy(cols(xr[:, c, 3:3 + NTOK]), wide(0)).then_inc(s_lev, 1)
                else:
                    A(cols(gel[:, c, :]), wide(3), ACT.Gelu_apprx_tanh).then_inc(s_lev, 1)
            high(U_OUT + 1)
            high(U_OUT + 2)
            for c in range(LT):
                xc, ga, gg, gt = lru_t
                act.wait_ge(s_gp, c + 1)
                if c >= 1:
                    act.wait_ge(s_lh, c)
                A(cols(ga[:]), wide(0), ACT.Sigmoid, bias=vec[:, V_BA + c:V_BA + c + 1]).then_inc(s_gs, 1)
                A(cols(gg[:]), wide(3), ACT.Sigmoid, bias=vec[:, V_BX + c:V_BX + c + 1]).then_inc(s_gs, 1)
                act.drain()
                A(gt[:], ga[:], ACT.Tanh, scale=nsp[:, 1, c:c + 1]).then_inc(s_ga, 1)
                act.drain()
                A(ga[:], ga[:], ACT.Exp, scale=nsp[:, 0, c:c + 1]).then_inc(s_ga, 1)
                act.wait_ge(s_lu, c + 1)
                A(gt[:], gt[:], ACT.Sqrt).then_inc(s_lq, 1)
            for i in range(NTT):
                act.wait_ge(s_kst, i + 1)
                act.wait_ge(s_kt, i + 1)
                nc.scalar.copy(kT[:, :, :, i * P:(i + 1) * P],
                               ps[:, 6 + i % 2, :].rearrange("p (k r t) -> p k r t", k=NKV, r=2)).then_inc(s_kte, 1)

            def q_high(i):
                act.wait_ge(s_kt, NTT) if i == 0 else act.wait_ge(s_qt, i)
                nc.scalar.copy(stk[:, :, 0, :].bitcast(F32R),
                               qk[:, i, 0:NH * HD].rearrange("p (h d) -> p h d", h=NH)).then_inc(s_qs, 1)

            def q_evac(i):
                act.wait_ge(s_qt, i + 1)
                if i >= 1:
                    act.wait_ge(s_lg, NH * i)
                nc.scalar.copy(qT[:], ps[:, 4:6, :].rearrange("p b (h t) -> p (b h) t", h=4)).then_inc(s_qte, 1)

            act.wait_ge(s_kvst, 64)
            for i in range(NTT):
                w = P * (i + 1)
                q_high(i)
                q_evac(i)
                for h in range(NH):
                    g = NH * i + h
                    act.wait_ge(s_lm, g + 1)
                    A(lg[g % 2][:, 0:w], lg[g % 2][:, 0:w], ACT.Exp, bias=nb[:, g % 2:g % 2 + 1], scale=SCALE,
                      accum_out=rsum[:, h:h + 1]).then_inc(s_ex, 1)
                act.wait_ge(s_ot, i + 1)
                nc.scalar.copy(attT[:, i, :, :], ps[:, 6 + i % 2, :].rearrange("p (c t) -> p c t", c=LT)
                               ).then_inc(s_ote, 1)
            for b in range(NB):
                act.wait_ge(s_dkt, b + 1)
                if b >= 2:
                    act.wait_ge(s_dlg, b)
                s = b % 2
                nc.scalar.copy(kbT[s][:, 0:1024], ps[:, 4:6, :].rearrange("p b n -> p (b n)")).then_inc(s_dke, 1)
                if b == 0:
                    act.wait_ge(s_dqe, 2)
                nc.scalar.copy(kbT[s][:, 1024:1025], knew[:, b:b + 1]).then_inc(s_dke, 1)
            act.wait_ge(s_dmx, 1)
            A(dlg[:], dlg[:], ACT.Exp, bias=dsm[:, 1:2], scale=SCALE, accum_out=dsm[:, 2:3]).then_inc(s_dex, 1)
            for n in range(8):
                if n >= 2:
                    act.wait_ge(s_gsu, n - 1)
                c = n % 4
                if n < 4:
                    if n == 0:
                        act.wait_ge(s_dat, 4)
                    A(nsq[n % 2][:], gel[:, c, :], ACT.Square).then_inc(s_gsq, 2)
                else:
                    A(nsq[n % 2][:, 0:T].rearrange("p (t n) -> p t n", t=NTT), attT[:, 0:NTT, c, :],
                      ACT.Square).then_inc(s_gsq, 1)
                    A(nsq[n % 2][:, T:NTOK], attT[:, NTT, c, 0:NB], ACT.Square).then_inc(s_gsq, 1)
            act.wait_ge(s_gv, 2)
            A(nr[0][:], nr[0][:], ACT.Sqrt).then_inc(s_gr, 1)
            A(nr[1][:], nr[1][:], ACT.Sqrt).then_inc(s_gr, 1)
            act.wait_ge(s_out, 16 * 5)
            for n in range(8):
                act.wait_ge(s_gt, n + 1)
                nc.scalar.copy(mixH[:, n, :], nt[:]).then_inc(s_gH, 1)
            for u in range(U_OUT + 3, U_FFN):
                high(u)
            for d in range(KD):
                if d == 0:
                    act.wait_ge(s_res, KD + 1)
                if d >= 2:
                    act.wait_ge(s_su2, d - 1)
                A(nsq[d % 2][:], xT[:, d, :], ACT.Square).then_inc(s_sq2, 1)
            act.wait_ge(s_v2, 1)
            A(nr[0][:], nr[0][:], ACT.Sqrt).then_inc(s_r2, 1)
            for d in range(KD):
                act.wait_ge(s_t2, d + 1)
                A(h2H[:, d, 0:T], nt[:, 0:T], ACT.Identity, bias=mod[:, 24 + d, 0:1]).then_inc(s_h2, 1)
            act.wait_ge(s_t2, KD + 1)
            nc.scalar.copy(h2H[:, :, T:NTOK], samp[:]).then_inc(s_h2, 1)

            act.drain().then_inc(s_sg, 1)
            with act.Fori(0, FB) as i:
                def high_ffn(k):
                    u = U_FFN + k
                    s = u % SLOTS
                    act.wait_ge(s_wr[s], i * 32 + 16 * (u // SLOTS + 1))
                    act.wait_ge(s_un, i * UPB + (u - SLOTS + 1))
                    nc.scalar.copy(wH[s][:], wraw[s][:]).then_inc(s_wH, 1)

                high_ffn(0)
                high_ffn(1)
                for f in range(2):
                    act.wait_ge(s_un, i * UPB + (U_FFN + 2 * f + 1))
                    act.wait_ge(s_af, i * 2 + (f + 1))
                    A(cols(sg[:]), wide(0), ACT.Silu).then_inc(s_sg, 1)
                    high_ffn(2 + 2 * f)
                    high_ffn(3 + 2 * f)
                    act.wait_ge(s_af, i * 2 + (f + 2))
                    if f == 0:
                        act.wait_ge(s_dn, i * 24 + 1)
                    nc.scalar.copy(aH[:, f, :], af[:]).then_inc(s_aH, 1)

            for i in range(ALLT):
                m = P if i < NTT else NB
                act.wait_ge(s_yt, 2 * i + 1)
                if i >= 2:
                    act.wait_ge(s_yst[i % 2], 16 * (i // 2))
                nc.scalar.copy(yo[i % 2][0:m, 0:512], ps[0:m, 2 * (i % 2), :]).then_inc(s_yea, 1)
                act.wait_ge(s_yt, 2 * i + 2)
                nc.scalar.copy(yo[i % 2][0:m, 512:D], ps[0:m, 2 * (i % 2) + 1, :]).then_inc(s_yea, 1)

        @block.vector
        def _(dve):
            V = nc.vector

            def stt(out, in0, scalar, in1, op0, op1):
                return V.scalar_tensor_tensor(out=out, in0=in0, scalar=scalar, in1=in1, op0=op0, op1=op1)

            for g in range(1, 16, 2):
                dve.wait_ge(s_tr, g + 1)
                i, hf = g // 2, g % 2
                V.tensor_copy(xT[:, 4 * hf:4 * hf + 4, i * P:(i + 1) * P],
                              ps[:, g % 4, :].rearrange("p (k t) -> p k t", k=4)).then_inc(s_xtv, 1)
            dve.wait_ge(s_mt, 1)
            V.tensor_copy(xT[:, :, T:NTOK], ps[:, 4, 0:64].rearrange("p (k b) -> p k b", k=KD)).then_inc(s_mte, 1)
            dve.wait_ge(s_mt, 2)
            V.tensor_copy(cT[:], ps[:, 7, 0:72].rearrange("p (k b) -> p k b", k=KD)).then_inc(s_mte, 1)
            dve.wait_ge(s_mt, 3)
            V.tensor_copy(vec[:], ps[:, 5, 0:V_ALL])
            V.tensor_copy(stT[:], ps[:, 5, 128:256])
            V.tensor_copy(gqk[:], ps[:, 5, 256:384].rearrange("p (g d) -> p g d", g=2))
            dve.drain()
            lam = vec[:, V_LAM:V_LAM + LT]
            stt(sp2[:, 0, :], lam, -1.0, lam, ALU.mult, ALU.max).then_inc(s_mte, 1)
            dve.wait_ge(s_modk, 12)
            V.tensor_tensor(mod[:], ps[:, 6, 0:432].rearrange("p (g b) -> p g b", b=1 + NB),
                            vec[:, V_ADA:V_ADA + 48].unsqueeze(2).to_broadcast([P, 48, 1 + NB]), ALU.add)
            dve.drain()

            def gains(row, scale_at):
                V.tensor_scalar(g1p[:], mod[:, scale_at:scale_at + KD, :], 1.0, None, ALU.add)
                dve.drain()
                V.tensor_tensor(g1p[:], g1p[:], vec[:, row:row + KD].unsqueeze(2).to_broadcast([P, KD, 1 + NB]),
                                ALU.mult)
                dve.drain()

            gains(V_LN1, 8)
            dve.wait_ge(s_squ, KD)

            def variance(dst, banks, n):
                V.tensor_scalar(cols(dst), wide(banks), 1.0 / n, EPS, ALU.mult, ALU.add)

            variance(rb[:], 0, D)
            dve.drain().then_inc(s_var, 1)
            dve.wait_ge(s_rt, 1)

            def modulated(rr, t, high_t, low_t, shift_at, s_t, s_h, s_l):
                V.reciprocal(rr[:], rr[:])
                dve.drain()
                for d in range(KD):
                    stt(t[:, 0:T], xT[:, d, 0:T], g1p[:, d, 0:1], rr[:, 0:T], ALU.mult, ALU.mult).then_inc(s_t, 1)
                    dve.wait_ge(s_h, d + 1)
                    stt(low_t[:, d, 0:T], t[:, 0:T], mod[:, shift_at + d, 0:1], high_t[:, d, 0:T].bitcast(F32),
                        ALU.add, ALU.subtract).then_inc(s_l, 1)
                    dve.drain()
                V.tensor_tensor(samp[:], xT[:, :, T:NTOK], g1p[:, :, 1:], ALU.mult)
                dve.drain()
                V.tensor_tensor(samp[:], samp[:], rr[:, T:NTOK].unsqueeze(1).to_broadcast([P, KD, NB]), ALU.mult)
                dve.drain()
                V.tensor_tensor(samp[:], samp[:], mod[:, shift_at:shift_at + KD, 1:], ALU.add).then_inc(s_t, 1)
                dve.wait_ge(s_h, KD + 1)
                V.tensor_tensor(low_t[:, :, T:NTOK], samp[:], high_t[:, :, T:NTOK].bitcast(F32),
                                ALU.subtract).then_inc(s_l, 1)

            modulated(rb, tt, hH, hL, 0, s_t, s_h, s_l)
            dve.drain()
            dve.wait_ge(s_modk, 12)
            V.memset(qk[:, NTT, :], 0.0)
            V.memset(iqk[:, NTT, :], 0.0)
            V.memset(vt[:, NTT, :], 0.0)
            dve.drain()
            V.memset(cnt[:], 0.0).then_inc(s_clr, 1)
            for n in range(1, 27, 2):
                j, i = n // 9, n % 9
                m = P if i < NTT else NB
                dve.wait_ge(s_pj, n + 1)
                if j == 0:
                    V.tensor_copy(iqk[0:m, i, :], ps[0:m, n % 6, 0:IQK]).then_inc(s_pjv, 1)
                elif j == 1:
                    V.tensor_copy(qk[0:m, i, 0:384], ps[0:m, n % 6, 0:384]).then_inc(s_pjv, 1)
                else:
                    V.tensor_copy(qk[0:m, i, 384:QK], ps[0:m, n % 6, 0:256])
                    dve.drain()
                    V.tensor_copy(vt[0:m, i, :], ps[0:m, n % 6, 256:384]).then_inc(s_pjv, 1)
            dve.drain()
            dve.wait_ge(s_pja, 19)

            rope = consts[:, C_ROPE:C_ALL].rearrange("p (t r) -> p t r", t=ALLT)

            def rotate(buf, c0, heads):
                v = buf[:, :, c0:c0 + heads * HD].rearrange("p t (h d) -> p t h d", h=heads)
                x1, x2 = v[:, :, :, 0:HALF], v[:, :, :, HALF:2 * HALF]
                cs = rope[:, :, 0:HALF].unsqueeze(2).to_broadcast([P, ALLT, heads, HALF])
                sn = rope[:, :, HALF:].unsqueeze(2).to_broadcast([P, ALLT, heads, HALF])
                t = [rt5[:, n, 0:ALLT * heads * HALF].rearrange("p (t h d) -> p t h d", t=ALLT, h=heads)
                     for n in range(4)]
                V.tensor_tensor(t[0], x1, cs, ALU.mult)
                V.tensor_tensor(t[1], x2, sn, ALU.mult)
                V.tensor_tensor(t[2], x2, cs, ALU.mult)
                V.tensor_tensor(t[3], x1, sn, ALU.mult)
                dve.drain()
                V.tensor_tensor(x1, t[0], t[1], ALU.subtract)
                last = V.tensor_tensor(x2, t[2], t[3], ALU.add)
                dve.drain()
                return last

            dve.wait_ge(s_pj, 27)
            rotate(iqk, 0, IH + 1)
            dve.drain().then_inc(s_iqr, 1)
            for i in range(NTT):
                s = i % 2
                dve.wait_ge(s_is, 3 * (i + 1))
                V.tensor_tensor(istk[s][:, :, 1, :].bitcast(F32R),
                                iqk[:, i, 0:IH * HD].rearrange("p (h d) -> p h d", h=IH), istk[s][:, :, 0, :],
                                ALU.subtract).then_inc(s_il, 1)
                V.tensor_tensor(ikstk[s][:, 1, :, :].bitcast(F32R),
                                iqk[:, i, IH * HD:IH * HD + HD].unsqueeze(1).to_broadcast([P, 2, HD]),
                                ikstk[s][:, 0, :, :], ALU.subtract).then_inc(s_il, 1)
                if i >= FIRST_SEL:
                    w = P * (i + 1)
                    sc = score[:, S_OFF[i]:S_OFF[i] + w]
                    for h in range(IH):
                        g = IH * (i - FIRST_SEL) + h
                        iw = iqk[:, i, IH * HD + HD + h:IH * HD + HD + h + 1]
                        dve.wait_ge(s_re, g + 1)
                        if h == 0:
                            V.tensor_scalar(sc, relu[g % 2][:, 0:w], iw, None, ALU.mult).then_inc(s_sa, 1)
                        else:
                            stt(sc, relu[g % 2][:, 0:w], iw, sc, ALU.mult, ALU.add).then_inc(s_sa, 1)
                        dve.drain()
                    V.tensor_tensor(sc[:, w - P:w], sc[:, w - P:w], caus, ALU.add)
                    dve.drain()
            V.memset(iqb[:], 0.0)
            dve.drain()
            dve.wait_ge(s_diw, 1)
            V.tensor_copy(iqb[:, :, 0:IH], ps[0:HD, 7, 0:32].rearrange("p (h b) -> p b h", h=IH))
            V.tensor_copy(iknew[:], ps[0:HD, 7, 32:40])
            V.tensor_tensor(iwc[:, 0:4], ps[0:32, 7, 64:68], consts[0:32, C_M4:C_M4 + 4], ALU.mult)
            dve.drain()
            V.tensor_reduce(iwc[:, 4:5], iwc[:, 0:4], AX.X, ALU.add)
            dve.drain()
            V.tensor_scalar(iwb[:], consts[0:32, C_E4T:C_E4T + 8], iwc[:, 4:5], None, ALU.mult).then_inc(s_diw, 1)
            for b in range(NB):
                dve.wait_ge(s_dit, b + 1)
                V.tensor_copy(ikb[b % 2][:, 0:1024],
                              ps[0:HD, 4:6, :].rearrange("p b n -> p (b n)")).then_inc(s_die, 1)
                V.tensor_copy(ikb[b % 2][:, 1024:1025], iknew[:, b:b + 1]).then_inc(s_die, 1)
            dve.wait_ge(s_dsc, 1)
            V.tensor_copy(score[0:NB, S_DEC:S_DEC + 1024], ps[0:NB, 4:6, :].rearrange("p b n -> p (b n)"))
            V.tensor_copy(score[0:NB, S_DEC + 1024:S_DEC + 1025], ps[0:NB, 6, 0:1])
            dve.wait_ge(s_qsq, 1)
            V.tensor_reduce(rstd[:], qsq[:].rearrange("p t (h d) -> p t h d", h=NH + NKV), AX.X, ALU.add)
            dve.drain()
            V.tensor_scalar(rstd[:], rstd[:], 1.0 / HD, EPS, ALU.mult, ALU.add).then_inc(s_qv, 1)
            dve.wait_ge(s_qr, 1)
            V.reciprocal(rstd[:], rstd[:])
            dve.drain()
            for i in range(ALLT):
                v = qk[:, i, :].rearrange("p (h d) -> p h d", h=NH + NKV)
                V.tensor_tensor(v, v, rstd[:, i, :].unsqueeze(2).to_broadcast([P, NH + NKV, HD]), ALU.mult)
            dve.drain()
            for i in range(ALLT):
                v = qk[:, i, :].rearrange("p (h d) -> p h d", h=NH + NKV)
                for g, (h0, h1) in enumerate(((0, NH), (NH, NH + NKV))):
                    V.tensor_tensor(v[:, h0:h1, :], v[:, h0:h1, :],
                                    gqk[:, g, :].unsqueeze(1).to_broadcast([P, h1 - h0, HD]), ALU.mult)
            dve.drain()
            rotate(qk, 0, NH + NKV)
            V.memset(keyK[:], 0)
            V.memset(keyX[:], 0)
            V.memset(keyC[:], -2147483648)
            V.memset(bit[:], 0x40000000)
            dve.drain().then_inc(s_qkr, 1)

            def count(op, thr):
                for n, (i, m, w, off) in enumerate(SEL):
                    V.tensor_scalar(junk[0:m, off:off + w], score[0:m, off:off + w], thr[0:m, n:n + 1].bitcast(F32), 0.0,
                                    op, ALU.add, accum_out=cnt[0:m, n:n + 1])
                dve.drain()

            def take():
                V.tensor_scalar(keep[:], cnt[:], float(TOPK), None, ALU.is_ge)
                dve.drain()
                V.copy_predicated(keyK[:], keep[:], keyC[:])
                dve.drain()

            dve.wait_ge(s_ikst, 32)
            count(ALU.is_ge, keyX)
            take()
            V.tensor_scalar(keyM[:], keyK[:], 31, None, ALU.arith_shift_right)
            dve.drain()
            V.tensor_scalar(keyM[:], keyM[:], -1, -2147483648, ALU.bitwise_xor, ALU.bitwise_or)
            dve.drain()
            with dve.Fori(0, 31) as _i:
                V.tensor_scalar(keyC[:], keyK[:], bit[:, 0:1], None, ALU.bitwise_or)
                stt(keyX[:], keyK[:], bit[:, 0:1], keyM[:], ALU.bitwise_or, ALU.bitwise_xor)
                dve.drain()
                V.tensor_scalar(bit[:], bit[:], 1, None, ALU.logical_shift_right)
                count(ALU.is_ge, keyX)
                take()
            V.tensor_tensor(keyX[:], keyK[:], keyM[:], ALU.bitwise_xor)
            dve.drain()
            count(ALU.is_gt, keyX)
            V.tensor_scalar(cnt[:], cnt[:], -1.0, float(TOPK), ALU.mult, ALU.add)
            dve.drain()
            for n, (i, m, w, off) in enumerate(SEL):
                thr = keyX[0:m, n:n + 1].bitcast(F32)
                sc = score[0:m, off:off + w]
                e, p = eqb[0:m, 0:w], preb[0:m, 0:w]
                V.tensor_scalar(e, sc, thr, None, ALU.is_equal)
                dve.drain()
                V.tensor_tensor_scan(p, e, e, 0.0, ALU.add, ALU.max)
                dve.drain()
                stt(e, p, cnt[0:m, n:n + 1], e, ALU.is_le, ALU.mult)
                dve.drain()
                stt(p, sc, thr, e, ALU.is_gt, ALU.add)
                dve.drain()
                V.tensor_scalar(sc, p, 1.0, -NEG, ALU.subtract, ALU.mult)
                dve.drain().then_inc(s_sel, 1)

            xc, ga, gg, gt = lru_t
            e_, z_, acc_ = sp2[:, 0, :], sp2[:, 1, :], sp2[:, 2, :]
            dve.wait_ge(s_exl, 1)
            V.tensor_scalar(z_, e_, 2.0, None, ALU.add)
            dve.drain()
            V.reciprocal(z_, z_)
            dve.drain()
            V.tensor_tensor(z_, z_, e_, ALU.mult)
            dve.drain()
            z2 = nsp[:, 2, :]
            V.tensor_tensor(z2, z_, z_, ALU.mult)
            V.memset(acc_, 1.0 / 19)
            dve.drain()
            for k in range(17, 0, -2):
                V.tensor_tensor(acc_, acc_, z2, ALU.mult)
                dve.drain()
                V.tensor_scalar(acc_, acc_, 1.0 / k, None, ALU.add)
                dve.drain()
            V.tensor_tensor(acc_, acc_, z_, ALU.mult)
            V.tensor_scalar(nsp[:, 3, :], lam, -1.0, 0.0, ALU.mult, ALU.max)
            dve.drain()
            stt(acc_, acc_, 2.0, nsp[:, 3, :], ALU.mult, ALU.add)
            dve.drain()
            V.tensor_scalar(nsp[:, 0, :], acc_, -C_LRU, None, ALU.mult)
            V.tensor_scalar(nsp[:, 1, :], acc_, C_LRU, None, ALU.mult)
            dve.drain()
            dve.wait_ge(s_lev, NU_LRU)
            V.memset(xr[:, :, 0:3], 0.0)
            dve.drain()
            for c in range(LT):
                cw = [vec[:, V_CW + 4 * i + c:V_CW + 4 * i + c + 1] for i in range(4)]
                cb = vec[:, V_CB + c:V_CB + c + 1]
                cst = stT[:, 32:128].rearrange("p (b i c) -> p b i c", b=NB, i=3)
                V.tensor_scalar(xc[:, 0:T], xr[:, c, 0:T], cw[0], cb, ALU.mult, ALU.add)
                V.tensor_scalar(xc[:, T:NTOK], cst[:, :, 0, c], cw[0], cb, ALU.mult, ALU.add)
                dve.drain()
                for i in range(1, 4):
                    last = stt(xc[:, 0:T], xr[:, c, i:i + T], cw[i], xc[:, 0:T], ALU.mult, ALU.add)
                    new = cst[:, :, i, c] if i < 3 else xr[:, c, 3 + T:3 + NTOK]
                    last = stt(xc[:, T:NTOK], new, cw[i], xc[:, T:NTOK], ALU.mult, ALU.add)
                    dve.drain()
                V.tensor_copy(lasts[:, 36 + c:48:4], xr[:, c, T:T + 3])
                V.tensor_copy(lasts[:, 48 + c:80:4], xr[:, c, 3 + T:3 + NTOK])
                dve.drain().then_inc(s_xc, 1)
                dve.wait_ge(s_ga, 2 * (c + 1))
                h = xr[:, c, 3:3 + NTOK]
                V.tensor_tensor(h, ga[:], ga[:], ALU.mult)
                dve.drain()
                stt(gt[:], h, 1.0, gt[:], ALU.add, ALU.mult).then_inc(s_lu, 1)
                V.tensor_tensor(gg[:], gg[:], xc[:], ALU.mult)
                dve.wait_ge(s_lq, c + 1)
                dve.drain()
                V.tensor_tensor(gg[:], gg[:], gt[:], ALU.mult)
                dve.drain()
                V.tensor_tensor_scan(h[:, 0:T], ga[:, 0:T], gg[:, 0:T], 0.0, ALU.mult, ALU.add)
                V.tensor_tensor(h[:, T:NTOK], ga[:, T:NTOK], stT[:, c:32:4], ALU.mult)
                dve.drain()
                V.tensor_tensor(h[:, T:NTOK], h[:, T:NTOK], gg[:, T:NTOK], ALU.add)
                dve.drain()
                V.tensor_copy(lasts[:, c:c + 1], h[:, T - 1:T])
                V.tensor_copy(lasts[:, 4 + c:36:4], h[:, T:NTOK])
                V.tensor_tensor(gel[:, c, :], gel[:, c, :], h, ALU.mult)
                dve.drain().then_inc(s_lh, 1)

            dve.wait_ge(s_lt, 1)
            V.tensor_copy(lrow[:], ps[0:80, 3, 0:P]).then_inc(s_lte, 1)

            kst = stk[:].rearrange("p h r d -> p (h r d)").rearrange("p (s k r c d) -> p s k r c d", s=2, k=NKV, r=2, c=2)
            for i in range(NTT):
                s = i % 2
                if i >= 2:
                    dve.wait_ge(s_kt, i - 1)
                for k in range(NKV):
                    kv = qk[:, i, (NH + k) * HD:(NH + k + 1) * HD].unsqueeze(1).to_broadcast([P, 2, HD])
                    V.tensor_copy(kst[:, s, k, 0].bitcast(F32R), kv)
                dve.drain()
                for k in range(NKV):
                    kv = qk[:, i, (NH + k) * HD:(NH + k + 1) * HD].unsqueeze(1).to_broadcast([P, 2, HD])
                    V.tensor_tensor(kst[:, s, k, 1].bitcast(F32R), kv, kst[:, s, k, 0], ALU.subtract)
                dve.drain().then_inc(s_kst, 1)

            def probs_evac(g):
                i = g // NH
                dve.wait_ge(s_ptt, g + 1)
                if g >= 2:
                    dve.wait_ge(s_pv, g - 1)
                V.tensor_copy(pT[g % 2][:, 0:i + 1, :],
                              ps[:, 4:6, :].rearrange("p b (k t) -> p (b k) t", k=4)[:, 0:i + 1, :]
                              ).then_inc(s_pte, 1)

            def heads(i):
                dve.wait_ge(s_ex, NH * (i + 1))
                V.reciprocal(rinv[:], rsum[:])
                dve.wait_ge(s_pv, NH * (i + 1))
                dve.drain()
                V.tensor_tensor(ob[:].rearrange("p (h d) -> p h d", h=NH),
                                ps[:, 6 + i % 2, :].rearrange("p (h d) -> p h d", h=NH),
                                rinv[:].unsqueeze(2).to_broadcast([P, NH, HD]), ALU.mult).then_inc(s_ob, 1)

            for i in range(NTT):
                w = P * (i + 1)
                dve.wait_ge(s_qs, i + 1)
                V.tensor_tensor(stk[:, :, 1, :].bitcast(F32R),
                                qk[:, i, 0:NH * HD].rearrange("p (h d) -> p h d", h=NH), stk[:, :, 0, :],
                                ALU.subtract).then_inc(s_ql, 1)
                for h in range(NH):
                    g = NH * i + h
                    s = g % 2
                    dve.wait_ge(s_lg, g + 1)
                    if g >= 2:
                        dve.wait_ge(s_ptt, g - 1)
                    src = ps[:, 2 * s:2 * s + 2, :].rearrange("p b n -> p (b n)")
                    if i >= FIRST_SEL:
                        V.tensor_tensor(lg[s][:, 0:w], src[:, 0:w], score[:, S_OFF[i]:S_OFF[i] + w], ALU.add)
                    else:
                        if w > P:
                            V.tensor_copy(lg[s][:, 0:w - P], src[:, 0:w - P])
                        V.tensor_tensor(lg[s][:, w - P:w], src[:, w - P:w], caus, ALU.add)
                    dve.drain()
                    V.tensor_reduce(mx[:, s:s + 1], lg[s][:, 0:w], AX.X, ALU.max)
                    dve.drain()
                    V.tensor_scalar(nb[:, s:s + 1], mx[:, s:s + 1], -SCALE, None, ALU.mult).then_inc(s_lm, 1)
                    if h >= 1:
                        probs_evac(g - 1)
                probs_evac(NH * i + NH - 1)
                heads(i)

            V.memset(qb[:], 0.0)
            dve.drain()
            dve.wait_ge(s_dqt, 1)
            dq = ps[:, 7, 0:32].rearrange("p (c b) -> p c b", c=4)
            for c in range(4):
                for par in range(2):
                    h, kv = 2 * c + par, c // 2
                    V.tensor_copy(qb[kv * 64:(kv + 1) * 64, :, h], dq[par * 64:(par + 1) * 64, c, :])
            dve.drain().then_inc(s_dqe, 1)
            V.tensor_copy(knew[:], ps[:, 7, 32:40]).then_inc(s_dqe, 1)
            dve.wait_ge(s_dlg, NB + 1)
            V.tensor_copy(dlg[:, 0:1024], ps[0:64, 0:2, :].rearrange("p b n -> p (b n)"))
            V.tensor_copy(dlg[:, 1024:1025], ps[0:64, 2, 0:1])
            dve.drain()
            V.tensor_reduce(dsm[:, 0:1], dlg[:], AX.X, ALU.max)
            dve.drain()
            V.tensor_scalar(dsm[:, 1:2], dsm[:, 0:1], -SCALE, None, ALU.mult).then_inc(s_dmx, 1)
            dve.wait_ge(s_dex, 1)
            V.reciprocal(dsm[:, 3:4], dsm[:, 2:3])
            dve.drain()
            V.tensor_scalar(dlg[:], dlg[:], dsm[:, 3:4], None, ALU.mult)
            dve.drain()
            V.tensor_scalar(ddg[:], consts[0:64, C_ID:C_ID + 64], dlg[:, 1024:1025], None, ALU.mult)
            dve.drain().then_inc(s_dpn, 1)
            dve.wait_ge(s_dpt, 1)
            V.tensor_copy(dpT[:], ps[:, 3, :].rearrange("p (g r) -> p g r", g=PG))
            V.tensor_copy(ptl[:], ps[0:NB, 4, 0:64])
            dve.drain().then_inc(s_dpe, 1)
            dve.wait_ge(s_dpu, NB)
            for kv in range(NKV):
                for par in range(2):
                    src = ps[kv * 64:(kv + 1) * 64, 5, 0:64].rearrange("p (b k c r) -> p k r c b", b=NB, k=NKV, c=2)
                    V.tensor_copy(attT[par * 64:(par + 1) * 64, NTT, 2 * kv:2 * kv + 2, 0:NB],
                                  src[:, kv, par]).then_inc(s_dat, 1)

            dve.wait_ge(s_gsu, 8)
            variance(nr[0][:], 0, LRU)
            variance(nr[1][:], 3, LRU)
            dve.drain().then_inc(s_gv, 2)
            dve.wait_ge(s_gr, 2)
            V.reciprocal(nr[0][:], nr[0][:])
            V.reciprocal(nr[1][:], nr[1][:])
            dve.drain()
            for n in range(8):
                c = n % 4
                gain = vec[:, (V_GL, V_GA)[n // 4] + c:(V_GL, V_GA)[n // 4] + c + 1]
                if n < 4:
                    stt(nt[:], gel[:, c, :], gain, nr[0][:], ALU.mult, ALU.mult).then_inc(s_gt, 1)
                else:
                    stt(nt[:, 0:T].rearrange("p (t n) -> p t n", t=NTT), attT[:, 0:NTT, c, :], gain,
                        nr[1][:, 0:T].rearrange("p (t n) -> p t n", t=NTT), ALU.mult, ALU.mult)
                    dve.drain()
                    stt(nt[:, T:NTOK], attT[:, NTT, c, 0:NB], gain, nr[1][:, T:NTOK],
                        ALU.mult, ALU.mult).then_inc(s_gt, 1)
                dve.wait_ge(s_gH, n + 1)
                V.tensor_tensor(mixL[:, n, :], nt[:], mixH[:, n, :].bitcast(F32), ALU.subtract).then_inc(s_gL, 1)
                dve.drain()
            gains(V_LN2, 32)
            dve.wait_ge(s_xback, 16)
            for n in range(KD):
                dve.wait_ge(s_un, U_OUT + n + 1)
                b0 = 3 * (n % 2)
                g1 = mod[:, 16 + n, 0:1]
                x3 = cols(xT[:, n, :])
                stt(x3[:, 0:2, :], ps[:, b0:b0 + 2, 0:CW], g1, x3[:, 0:2, :], ALU.mult, ALU.add)
                stt(x3[:, 2, 0:TAIL], ps[:, b0 + 2, 0:TAIL], g1, x3[:, 2, 0:TAIL], ALU.mult, ALU.add)
                V.tensor_copy(samp[:, n, :], ps[:, b0 + 2, TAIL:CW])
                dve.drain().then_inc(s_res, 1)

            def sample_residual(gate_at, src):
                V.tensor_tensor(src[:], src[:], mod[:, gate_at:gate_at + KD, 1:], ALU.mult)
                dve.drain()
                V.tensor_tensor(xT[:, :, T:NTOK], xT[:, :, T:NTOK], src[:], ALU.add)
                dve.drain()

            sample_residual(16, samp)
            dve.drain().then_inc(s_res, 1)
            dve.wait_ge(s_su2, KD)
            variance(nr[0][:], 0, D)
            dve.drain()
            V.memset(samp2[:], 0.0).then_inc(s_v2, 1)
            dve.wait_ge(s_r2, 1)
            modulated(nr[0], nt, h2H, h2L, 24, s_t2, s_h2, s_l2)
            dve.drain()

            dve.drain().then_inc(s_af, 1)
            dve.drain().then_inc(s_dne, 1)
            with dve.Fori(0, FB) as i:
                for f in range(2):
                    dve.wait_ge(s_sg, i * 2 + (f + 2))
                    dve.wait_ge(s_un, i * UPB + (U_FFN + 2 * f + 2))
                    V.tensor_tensor(cols(af[:]), wide(3), cols(sg[:]), ALU.mult).then_inc(s_af, 1)
                    dve.wait_ge(s_aH, i * 2 + (f + 1))
                    V.tensor_tensor(aL[:, f, :], af[:], aH[:, f, :].bitcast(F32), ALU.subtract).then_inc(s_aL, 1)
                    dve.drain()
                for n in range(KD):
                    for c in range(NCH):
                        q = n * NCH + c
                        w = CW if c < 2 else TAIL
                        dve.wait_ge(s_dn, i * 24 + (q + 2))
                        xp = xT[:, n, c * CW:c * CW + w]
                        ins = stt(xp, ps[:, 6 + q % 2, 0:w], mod[:, 40 + n, 0:1], xp, ALU.mult, ALU.add)
                        if c == 2:
                            ins = V.tensor_tensor(samp2[:, n, :], samp2[:, n, :], ps[:, 6 + q % 2, TAIL:CW], ALU.add)
                            dve.drain().then_inc(s_dne, 1)
                        else:
                            ins.then_inc(s_dne, 1)
                dve.drain()
            sample_residual(40, samp2)
            dve.drain().then_inc(s_y, 1)

        @block.tensor
        def _(pe):
            mm, tr = pe.matmul, pe.transpose

            pe.wait_ge(s_const, 16)
            for i in range(NTT):
                pe.wait_ge(s_x[i], 16)
                for hf in range(2):
                    g = 2 * i + hf
                    if g >= 4:
                        pe.wait_ge((s_xta, s_xtv)[g % 2], (g - 4) // 2 + 1)
                    for k in range(4):
                        ins = tr(ps[:, g % 4, k * P:(k + 1) * P], xin[:, i, (4 * hf + k) * P:(4 * hf + k + 1) * P],
                                 ident)
                    ins.then_inc(s_tr, 1)
            pe.wait_ge(s_small, 16 * 18)
            for k in range(KD):
                ins = tr(ps[:, 4, k * 8:k * 8 + 8], xs_in[:, k * P:(k + 1) * P], ident[0:NB, 0:NB])
            ins.then_inc(s_mt, 1)
            pe.wait_ge(s_csi, 1)
            for k in range(KD):
                ins = tr(ps[:, 7, k * 9:9 + k * 9], c_si[:, k * P:(k + 1) * P], ident[0:9, 0:9])
            ins.then_inc(s_mt, 1)
            tr(ps[:, 5, 0:V_ALL], vrows[:], ident[0:V_ALL, 0:V_ALL])
            tr(ps[:, 5, 128:256], strows[:], ident)
            mm(ps[:, 5, 256:384], ones[0:1, :], grow[0:1, :], start=True, stop=True).then_inc(s_mt, 1)
            pe.wait_ge(s_mte, 2)
            for j in range(12):
                pe.wait_ge(s_ada[j % 4], 16 * (j // 4 + 1))
                for q in range(4):
                    g = 4 * j + q
                    for k in range(KD):
                        ins = mm(ps[:, 6, g * 9:g * 9 + 9], ada[j % 4][:, k, q * P:(q + 1) * P], cT[:, k, :],
                                 start=(k == 0), stop=(k == KD - 1))
                ins.then_inc(s_modk, 1)

            def stats(src, ready, used, b0, n, first=0, per=1):
                for d in range(n):
                    pe.wait_ge(ready, per * (first + d + 1))
                    for c in range(NCH):
                        ins = mm(ps[:, b0 + c, 0:CW], ones, src[(first + d) % 2][:, c * CW:(c + 1) * CW],
                                 start=(d == 0), stop=(d == n - 1))
                    ins.then_inc(used, 1)

            stats(sq, s_sq, s_squ, 0, KD)
            pe.wait_ge(s_l, KD + 1)
            for n in range(27):
                j, i = n // 9, n % 9
                m = P if i < NTT else NB
                w = CHUNKS[j][1]
                if i == 0:
                    pe.wait_ge(s_cL, j + 1)
                if n >= 6:
                    q = n - 6
                    if q % 2:
                        pe.wait_ge(s_pjv, q // 2 + 1)
                    else:
                        pe.wait_ge(s_pja, q // 2 + 1 + (q // 2 - 8 if q >= 18 else 0))
                t0 = i * P
                for k in range(KD):
                    hi, lo = hH[:, k, t0:t0 + m], hL[:, k, t0:t0 + m]
                    wh, wl = cH[j % 2][:, k, 0:w], cL[j % 2][:, k, 0:w]
                    dst = ps[0:m, n % 6, 0:w]
                    mm(dst, hi, wh, start=(k == 0), stop=False)
                    mm(dst, hi, wl, start=False, stop=False)
                    ins = mm(dst, lo, wh, start=False, stop=(k == KD - 1))
                ins.then_inc(s_pj, 1)
            pe.wait_ge(s_pja, 19)
            pe.wait_ge(s_pjv, 13)

            def index_scores(i):
                for h in range(IH):
                    g = IH * (i - FIRST_SEL) + h
                    if h == 0:
                        pe.wait_ge(s_ite, i + 1)
                        pe.wait_ge(s_ikte, i + 1)
                    if g >= 2:
                        pe.wait_ge(s_re, g - 1)
                    for n0, n in halves(P * (i + 1)):
                        dst = ps[:, 2 * (g % 2) + n0 // 512, 0:n]
                        mm(dst, iqT[i % 2][:, h, :], ikT[:, 0, n0:n0 + n], start=True, stop=False)
                        ins = mm(dst, iqT[i % 2][:, h, :], ikT[:, 1, n0:n0 + n], start=False, stop=True)
                    ins.then_inc(s_sc, 1)

            for i in range(NTT):
                s = i % 2
                pe.wait_ge(s_il, 2 * (i + 1))
                if i >= 2:
                    pe.wait_ge(s_ite, i - 1)
                    pe.wait_ge(s_ikte, i - 1)
                for h in range(IH):
                    tr(ps[:, 4 + s, h * P:(h + 1) * P], istk[s][:, h].rearrange("p r d -> p (r d)"), ident)
                for r in range(2):
                    ins = tr(ps[:, 6 + s, r * P:(r + 1) * P], ikstk[s][:, r].rearrange("p c d -> p (c d)"), ident)
                ins.then_inc(s_it, 1)
                if i >= FIRST_SEL:
                    index_scores(i)
            pe.wait_ge(s_ikte, NTT)
            for h in range(IH):
                tr(ps[0:HD, 7, h * 8:h * 8 + 8], iqk[0:NB, NTT, h * HD:(h + 1) * HD], ident[0:NB, 0:NB])
            tr(ps[0:HD, 7, 32:40], iqk[0:NB, NTT, IH * HD:IH * HD + HD], ident[0:NB, 0:NB])
            mm(ps[0:32, 7, 64:68], consts[0:NB, C_E4:C_E4 + 32], iqk[0:NB, NTT, IH * HD + HD:IQK],
               start=True, stop=True).then_inc(s_diw, 1)
            pe.wait_ge(s_re, IH * (NTT - FIRST_SEL))

            def decode_index(b):
                pe.wait_ge(s_die, 2 * (b + 1))
                if b == 0:
                    pe.wait_ge(s_diw, 2)
                for c, (n0, n) in enumerate(halves(NKEY)):
                    ins = mm(ps[0:32, c, 0:n], iqb[:].rearrange("p b k -> p (b k)")[:, 32 * b:32 * b + 32],
                             ikb[b % 2][:, n0:n0 + n], start=(b == 0), stop=(b == NB - 1))
                return ins

            for b in range(NB):
                pe.wait_ge(s_ipg[b % 2], 16 * PG * (b // 2 + 1))
                if b >= 1:
                    pe.wait_ge(s_die, 2 * b)
                for g in range(PG):
                    ins = tr(ps[0:HD, 4 + g // 4, (g % 4) * P:(g % 4 + 1) * P], ipg[b % 2][:, g, :], ident)
                if b >= 1:
                    ins = decode_index(b - 1)
                ins.then_inc(s_dit, 1)
            decode_index(NB - 1).then_inc(s_dis, 1)
            pe.wait_ge(s_dir, 2)
            for c, (n0, n) in enumerate(halves(NKEY)):
                ins = mm(ps[0:NB, 4 + c, 0:n], iwb[:], reld[:, n0:n0 + n], start=True, stop=True)
            ins.then_inc(s_dsc, 1)
            pe.wait_ge(s_qsq, 1)

            def unit(u, hi, lo, b0):
                s = u % SLOTS
                for k in range(KD):
                    for c in range(NCH):
                        cc = slice(c * CW, (c + 1) * CW)
                        dst = ps[:, b0 + c, 0:CW]
                        mm(dst, wH[s][:, k, :], hi[:, k, cc], start=(k == 0), stop=False)
                        mm(dst, wH[s][:, k, :], lo[:, k, cc], start=False, stop=False)
                        ins = mm(dst, wL[s][:, k, :], hi[:, k, cc], start=False, stop=(k == KD - 1))
                ins.then_inc(s_un, 1)

            pe.wait_ge(s_qkr, 1)
            for u in range(NU_LRU):
                pe.wait_ge(s_wL, u + 1)
                if u >= 2:
                    pe.wait_ge(s_lev, u - 1)
                unit(u, hH, hL, 3 * (u % 2))
            pe.wait_ge(s_lev, NU_LRU)
            pe.wait_ge(s_wbd, 64)
            for c in range(LT):
                pe.wait_ge(s_xc, c + 1)
                if c >= 1:
                    pe.wait_ge(s_gs, 2 * c)
                for gate in range(2):
                    for n in range(NCH):
                        ins = mm(ps[:, 3 * gate + n, 0:CW], wbd[:, gate, c, :], lru_t[0][:, n * CW:(n + 1) * CW],
                                 start=True, stop=True)
                ins.then_inc(s_gp, 1)
            pe.wait_ge(s_lh, LT)
            tr(ps[0:80, 3, 0:P], lasts[:], ident).then_inc(s_lt, 1)
            kst = stk[:].rearrange("p h r d -> p (h r d)").rearrange("p (s k r n) -> p s k r n", s=2, k=NKV, r=2)
            for i in range(NTT):
                pe.wait_ge(s_kst, i + 1)
                if i >= 2:
                    pe.wait_ge(s_kte, i - 1)
                for k in range(NKV):
                    for r in range(2):
                        n = 2 * k + r
                        ins = tr(ps[:, 6 + i % 2, n * P:(n + 1) * P], kst[:, i % 2, k, r, :], ident)
                ins.then_inc(s_kt, 1)
            pe.wait_ge(s_kte, NTT)
            pe.wait_ge(s_lte, 1)

            def logits(g):
                i, h = g // NH, g % NH
                if h == 0:
                    pe.wait_ge(s_ql, i + 1)
                    if g >= 1:
                        pe.wait_ge(s_pte, g)
                    for q in range(NH):
                        ins = tr(ps[:, 4 + q // 4, (q % 4) * P:(q % 4 + 1) * P],
                                 stk[:, q].rearrange("p r d -> p (r d)"), ident)
                    ins.then_inc(s_qt, 1)
                    pe.wait_ge(s_qte, i + 1)
                if g >= 2:
                    pe.wait_ge(s_lm, g - 1)
                for n0, n in halves(P * (i + 1)):
                    dst = ps[:, 2 * (g % 2) + n0 // 512, 0:n]
                    mm(dst, qT[:, h, :], kT[:, h // GRP, 0, n0:n0 + n], start=True, stop=False)
                    ins = mm(dst, qT[:, h, :], kT[:, h // GRP, 1, n0:n0 + n], start=False, stop=True)
                ins.then_inc(s_lg, 1)

            def transposed(g):
                i = g // NH
                pe.wait_ge(s_ex, g + 1)
                if g >= 1:
                    pe.wait_ge(s_pte, g)
                for k in range(i + 1):
                    ins = tr(ps[:, 4 + k // 4, (k % 4) * P:(k % 4 + 1) * P], lg[g % 2][:, k * P:(k + 1) * P], ident)
                ins.then_inc(s_ptt, 1)

            def mixed(g):
                i, h = g // NH, g % NH
                kv = h // GRP
                pe.wait_ge(s_pte, g + 1)
                if h == 0 and i >= 2:
                    pe.wait_ge(s_ote, i - 1)
                for k in range(i + 1):
                    ins = mm(ps[:, 6 + i % 2, h * HD:(h + 1) * HD], pT[g % 2][:, k, :],
                             vt[:, k, kv * HD:(kv + 1) * HD], start=(k == 0), stop=(k == i))
                ins.then_inc(s_pv, 1)

            for i in range(NTT):
                logits(NH * i)
                for h in range(NH):
                    g = NH * i + h
                    if h < NH - 1:
                        logits(g + 1)
                    transposed(g)
                    mixed(g)
                pe.wait_ge(s_ob, i + 1)
                for c in range(LT):
                    ins = tr(ps[:, 6 + i % 2, c * P:(c + 1) * P], ob[:, c * P:(c + 1) * P], ident)
                ins.then_inc(s_ot, 1)

            pe.wait_ge(s_ote, NTT)
            for c in range(4):
                tr(ps[:, 7, c * 8:c * 8 + 8], qk[0:NB, NTT, c * P:(c + 1) * P], ident[0:NB, 0:NB])
            tr(ps[:, 7, 32:40], qk[0:NB, NTT, NH * HD:QK], ident[0:NB, 0:NB]).then_inc(s_dqt, 1)
            pe.wait_ge(s_sel, 1)
            for c, (n0, n) in enumerate(halves(NKEY)):
                ins = mm(ps[0:64, c, 0:n], consts[0:NB, C_E8:C_E8 + 64], score[0:NB, S_DEC + n0:S_DEC + n0 + n],
                         start=True, stop=False)
            ins.then_inc(s_dlg, 1)

            def decode_logits(b):
                pe.wait_ge(s_dke, 2 * (b + 1))
                for c, (n0, n) in enumerate(halves(NKEY)):
                    ins = mm(ps[0:64, c, 0:n], qb[:].rearrange("p b k -> p (b k)")[:, 64 * b:64 * b + 64],
                             kbT[b % 2][:, n0:n0 + n], start=False, stop=(b == NB - 1))
                ins.then_inc(s_dlg, 1)

            pe.wait_ge(s_dqe, 1)
            for b in range(NB):
                pe.wait_ge(s_kpg[b % 2], 16 * PG * (b // 2 + 1))
                if b >= 1:
                    pe.wait_ge(s_dke, 2 * b)
                for g in range(PG):
                    ins = tr(ps[:, 4 + g // 4, (g % 4) * P:(g % 4 + 1) * P], kpg[b % 2][:, g, :], ident)
                ins.then_inc(s_dkt, 1)
                if b >= 1:
                    decode_logits(b - 1)
            decode_logits(NB - 1)
            pe.wait_ge(s_dpn, 1)
            for g in range(PG):
                tr(ps[:, 3, g * 64:(g + 1) * 64], dlg[:, g * P:(g + 1) * P], ident[0:64, 0:64])
            mm(ps[0:NB, 4, 0:64], consts[0:64, C_E8T:C_E8T + NB], ddg[:], start=True, stop=True).then_inc(s_dpt, 1)
            pe.wait_ge(s_dpe, 1)
            mm(ps[:, 5, 0:64], vt[0:NB, NTT, :], ptl[:], start=True, stop=False, skip_group_check=True)
            for b in range(NB):
                pe.wait_ge(s_vpg[b % 2], 16 * PG * (b // 2 + 1))
                for g in range(PG):
                    ins = mm(ps[:, 5, 8 * b:8 * b + 8], vpg[b % 2][:, g, :], dpT[:, g, 8 * b:8 * b + 8],
                             start=False, stop=(g == PG - 1), skip_group_check=True)
                ins.then_inc(s_dpu, 1)

            stats(nsq, s_gsq, s_gsu, 0, 4, first=0, per=2)
            stats(nsq, s_gsq, s_gsu, 3, 4, first=4, per=2)
            pe.wait_ge(s_gL, 8)
            for n in range(NU_OUT):
                u = U_OUT + n
                pe.wait_ge(s_wL, u + 1)
                if n >= 2:
                    pe.wait_ge(s_res, n - 1)
                unit(u, mixH, mixL, 3 * (n % 2))
            stats(nsq, s_sq2, s_su2, 0, KD)
            pe.wait_ge(s_l2, KD + 1)

            pe.sem_inc(s_dn, 1)
            with pe.Fori(0, FB) as i:
                for k in range(4):
                    u = U_FFN + k
                    pe.wait_ge(s_wL, i * UPB + (u + 1))
                    if k % 2 == 0:
                        pe.wait_ge(s_sg, i * 2 + (k // 2 + 1))
                    else:
                        pe.wait_ge(s_af, i * 2 + (k // 2 + 1))
                    unit(u, h2H, h2L, 3 * (k % 2))
                pe.wait_ge(s_wL, i * UPB + (U_FFN + 6))
                pe.wait_ge(s_aL, i * 2 + 2)
                for n in range(KD):
                    for c in range(NCH):
                        q = n * NCH + c
                        if q >= 2:
                            pe.wait_ge(s_dne, i * 24 + q)
                        else:
                            pe.wait_ge(s_dne, i * 24 + 1)
                        dst = ps[:, 6 + q % 2, 0:CW]
                        cc = slice(c * CW, (c + 1) * CW)
                        for f in range(2):
                            s = (U_FFN + 4 + f) % SLOTS
                            mm(dst, wH[s][:, n, :], aH[:, f, cc], start=(f == 0), stop=False)
                            mm(dst, wH[s][:, n, :], aL[:, f, cc], start=False, stop=False)
                            ins = mm(dst, wL[s][:, n, :], aH[:, f, cc], start=False, stop=(f == 1))
                        ins.then_inc(s_dn, 1)
                pe.wait_ge(s_dn, i * 24 + 25)
                for f in range(2):
                    pe.sem_inc(s_un, 1)

            pe.wait_ge(s_y, 1)
            for i in range(ALLT):
                m = P if i < NTT else NB
                for hf in range(2):
                    if i >= 2:
                        pe.wait_ge(s_yea, 2 * (i - 2) + hf + 1)
                    for k in range(4):
                        ins = tr(ps[0:m, 2 * (i % 2) + hf, k * P:(k + 1) * P], xT[:, 4 * hf + k, i * P:i * P + m],
                                 ident)
                    ins.then_inc(s_yt, 1)


_INS = ['x_prompt', 'x_sample', 'cache_k', 'cache_v', 'cache_ik', 'state_h', 'state_conv', 'page_table',
        'c_prompt', 'c_sample', 'ada_w', 'ada_b', 'ln1_g', 'w_in', 'conv_w', 'conv_b', 'lru_wa', 'lru_ba',
        'lru_wx', 'lru_bx', 'lru_lambda', 'q_norm_g', 'k_norm_g', 'gn_lru_g', 'gn_att_g', 'w_out', 'ln2_g',
        'w_gate', 'w_up', 'w_down']
_OUTS = [('y_prompt', (1, T, D)), ('y_sample', (NB, 1, D)),
         ('k_prompt', (1, 1, T, NKV, HD)), ('v_prompt', (1, 1, T, NKV, HD)), ('ik_prompt', (1, 1, T, HD)),
         ('h_prompt', (1, 1, LRU)), ('conv_prompt', (1, 1, 3, LRU)),
         ('k_sample', (1, NB, 1, NKV, HD)), ('v_sample', (1, NB, 1, NKV, HD)), ('ik_sample', (1, NB, 1, HD)),
         ('h_sample', (1, NB, LRU)), ('conv_sample', (1, NB, 3, LRU))]


def table():
    c = np.zeros((P, C_ALL), np.float32)
    r = np.arange(P)
    c[:, C_ID:C_ID + P] = np.eye(P)
    c[:, C_CAUS:C_CAUS + P] = np.where(r[None, :] <= r[:, None], 0.0, -3.0e38)
    c[:, C_ONE:C_ONE + P] = 1.0
    c[0:8, C_E4:C_E4 + 32] = np.repeat(np.eye(8), 4, axis=1)
    c[0:32, C_E4T:C_E4T + 8] = np.repeat(np.eye(8), 4, axis=0)
    c[0:32, C_M4:C_M4 + 4] = np.tile(np.eye(4), (8, 1))
    c[0:8, C_E8:C_E8 + 64] = np.repeat(np.eye(8), 8, axis=1)
    c[0:64, C_E8T:C_E8T + 8] = np.repeat(np.eye(8), 8, axis=0)
    freq = (np.float32(500000.0) ** (-np.arange(HALF, dtype=np.float32) / np.float32(HALF))).astype(np.float32)
    pos = np.full((ALLT, P), T, np.float32)
    pos[:NTT] = np.arange(T).reshape(NTT, P)
    ang = (pos[:, :, None] * freq).astype(np.float32).astype(np.float64)
    rope = np.concatenate([np.cos(ang), np.sin(ang)], axis=-1)
    c[:, C_ROPE:] = rope.transpose(1, 0, 2).reshape(P, -1)
    return c


def kernel(**inputs):
    import numpy as _np
    import concourse.bacc as _bacc
    from concourse import mybir as _mybir
    from concourse.bass_utils import run_bass_kernel_spmd as _run

    nc = _bacc.Bacc("TRN2", target_bir_lowering=False, num_devices=1)
    arrays, ins, outs = {}, {}, {}
    for name in _INS:
        x = _np.ascontiguousarray(inputs[name])
        arrays["in_" + name] = x
        ins[name] = nc.dram_tensor("in_" + name, x.shape, _mybir.dt.from_np(x.dtype), kind="ExternalInput").ap()
    x = table()
    arrays["in_consts"] = x
    ins["consts"] = nc.dram_tensor("in_consts", x.shape, _mybir.dt.from_np(x.dtype), kind="ExternalInput").ap()
    for name, shape in _OUTS:
        outs[name] = nc.dram_tensor("out_" + name, shape, _mybir.dt.float32, kind="ExternalOutput").ap()
    build(nc, ins, outs)
    r = _run(nc, [arrays], core_ids=[0])
    return tuple(r.results[0]["out_" + name] for name, _ in _OUTS)
```

```python
from contextlib import ExitStack

import numpy as np

import concourse.bass as bass
from concourse import mybir

P = 128
ALU = mybir.AluOpType
ACT = mybir.ActivationFunctionType
AX = mybir.AxisListType
F32 = mybir.dt.float32
F32R = mybir.dt.float32r
BF16 = mybir.dt.bfloat16
I32 = mybir.dt.int32

D = 1024
KD = D // P
T = 1024
NB = 8
NTOK = T + NB
NCH = 3
CW = NTOK // NCH
TAIL = CW - NB
NTT = T // P
ALLT = NTT + 1
LRU = 512
LT = LRU // P
NH, NKV, HD = 8, 2, 64
GRP = NH // NKV
IH = 4
TOPK = 256
QK = NH * HD + NKV * HD
IQK = IH * HD + HD + IH
HALF = 8
PG = 8
NPOOL = 80
NKEY = PG * P + 1
DFF = 2816
FT = DFF // P
EPS = 1e-6
C_LRU = 8.0
SCALE = HD ** -0.5
NEG = -1.0e30
FIRST_SEL = TOPK // P

C_ID, C_CAUS, C_ONE, C_E4, C_E4T, C_M4, C_E8, C_E8T, C_ROPE = 0, 128, 256, 384, 416, 424, 428, 492, 500
C_ALL = C_ROPE + ALLT * 2 * HALF

V_LN1, V_LN2, V_CW, V_CB, V_BA, V_BX, V_LAM, V_GL, V_GA, V_ADA = 0, 8, 16, 32, 36, 40, 44, 48, 52, 56
V_ALL = 104

CHUNKS = [(1792, IQK), (1024, 384), (1408, 384)]

NU_LRU, NU_OUT = 8, 8
U_OUT = NU_LRU
U_FFN = NU_LRU + NU_OUT
FB = FT // 2
UPB = 6
SLOTS = 3
U_ALL = U_FFN + FB * UPB

S_OFF = {}
_o = 0
for _i in range(FIRST_SEL, NTT):
    S_OFF[_i] = _o
    _o += P * (_i + 1)
S_DEC = _o
S_ALL = _o + NKEY
SEL = [(i, P, P * (i + 1), S_OFF[i]) for i in range(FIRST_SEL, NTT)] + [(NTT, NB, NKEY, S_DEC)]
NSEL = len(SEL)
SEL_ACT = 4
KEY_BITS = 32


NG = NTT * NKV


def tile_of(n):
    return n // NKV


def first_item(n):
    return 1 + key_count(n) + min(n + 1, NG - 1)


def q_item(n):
    return 0 if n == 0 else first_item(n - 1) - 1


def key_count(n):
    return sum(tile_of(q) + 1 for q in range(n))


def halves(w):
    return [(a, min(512, w - a)) for a in range(0, w, 512)]


def build(nc, a, o):
    ctx = ExitStack()
    with ctx:
        def sb(name, shape, dt=F32):
            return ctx.enter_context(nc.sbuf_tensor(name, shape, dt))

        def sem(name):
            return ctx.enter_context(nc.semaphore(name))

        consts = sb("consts", [P, C_ALL])
        ident = consts[:, C_ID:C_ID + P]
        caus = consts[:, C_CAUS:C_CAUS + P]
        ones = consts[:, C_ONE:C_ONE + P]
        vec = sb("vec", [P, V_ALL])
        stT = sb("stT", [P, P])
        gqk = sb("gqk", [P, 2, HD])
        mod = sb("mod", [P, 48, 1 + NB])
        g1p = sb("g1p", [P, KD, 1 + NB])
        wbd = sb("wbd", [P, 2, LT, P])
        nsp = sb("nsp", [P, 4, LT])
        sp2 = sb("sp2", [P, 3, LT])
        pt_sb = sb("pt_sb", [1, NB * PG], I32)
        lasts = sb("lasts", [P, 80])
        keyK = sb("keyK", [P, NSEL], I32)
        keyC = sb("keyC", [P, NSEL], I32)
        keyX = sb("keyX", [P, NSEL], I32)
        keyM = sb("keyM", [P, NSEL], I32)
        keep = sb("keep", [P, NSEL], I32)
        keyN = sb("keyN", [P, NSEL], I32)
        keyL = sb("keyL", [P, 2, NSEL], I32)
        bit = sb("bit", [P, 1], I32)
        limit = sb("limit", [P, NSEL])
        cnt = sb("cnt", [P, NSEL])
        rstd = sb("rstd", [P, ALLT, NH + NKV])
        nb = sb("nb", [P, 2 * GRP])
        dsm = sb("dsm", [64, 8])
        iwc = sb("iwc", [32, 8])
        iwb = sb("iwb", [32, NB])
        samp = sb("samp", [P, KD, NB])
        samp2 = sb("samp2", [P, KD, NB])

        base = nc.sbuf_base
        RH, RP = base, base + 2 * KD * NTOK * 4
        size = 2 * KD * NTOK * 4 + 133504
        ctx.enter_context(nc.sbuf_tensor("arena", [P, size // 4], F32))

        def at(name, shape, off, dt=F32):
            return nc.alloc_sbuf_tensor_at(name, shape, dt, offset=off)

        A_X = RP + 100480
        hH = at("hH", [P, KD, NTOK], RH, F32R)
        hL = at("hL", [P, KD, NTOK], RH + KD * NTOK * 4, F32R)
        xin = at("xin", [P, NTT, D], RH)
        xT = at("xT", [P, KD, NTOK], A_X)
        ada = [at(f"ada{i}", [P, KD, 512], RP + 16384 * i) for i in range(4)]
        sq = [at(f"sq{i}", [P, NTOK], RP + 65600 + 4160 * i) for i in range(2)]
        rb = at("rb", [P, NTOK], RP + 73920)
        tt = at("tt", [P, NTOK], RP + 78080)
        xs_in = at("xs_in", [NB, D], RP + 82240)
        c_in = at("c_in", [1 + NB, D], RP + 86336)
        c_si = at("c_si", [1 + NB, D], RP + 90432)
        cT = at("cT", [P, KD, 1 + NB], RP + 94528)
        vrows = at("vrows", [V_ALL, P], RP + 94848)
        strows = at("strows", [P, P], RP + 95360)
        grow = at("grow", [1, P], RP + 95872)
        qk = at("qk", [P, ALLT, QK], RP)
        vt = at("vt", [P, ALLT, P], RP + 23040)
        iqk = at("iqk", [P, ALLT, IQK], RP + 27648)
        craw = [at("craw0", [P, KD, 384], RP + 83200), at("craw1", [P, KD, 384], RP + 39328)]
        cH = [at("cH0", [P, KD, 384], RP + 51616, F32R), at("cH1", [P, KD, 384], RP + 95488, F32R)]
        cL = [at("cL0", [P, KD, 384], RP + 63904, F32R), at("cL1", [P, KD, 384], RP + 107776, F32R)]
        score = at("score", [P, S_ALL], RP + 39328)
        RING = RP + 60352
        wraw = [at(f"wraw{i}", [P, KD, P], RING + 4096 * i) for i in range(SLOTS)]
        wH = [at(f"wH{i}", [P, KD, P], RING + 12288 + 8192 * i, F32R) for i in range(SLOTS)]
        wL = [at(f"wL{i}", [P, KD, P], RING + 12288 + 8192 * i + 4096, F32R) for i in range(SLOTS)]
        Q5 = RING + 36864
        ikT = at("ikT", [P, 2, T], Q5, F32R)
        istk = [at(f"istk{i}", [P, IH, 2, HD], Q5 + 8192 + 3072 * i) for i in range(2)]
        ikstk = [at(f"ikstk{i}", [P, 2, 2, HD], Q5 + 10240 + 3072 * i) for i in range(2)]
        iqT = [at(f"iqT{i}", [P, IH, P], Q5 + 14336 + 2048 * i, F32R) for i in range(2)]
        relu = [at(f"relu{i}", [P, T], Q5 + 18432 + 4096 * i) for i in range(2)]
        rt5 = at("rt5", [P, 4, ALLT * (NH + NKV) * HALF], RING)
        ipg = [at(f"ipg{i}", [P, PG, HD], RING + 12288 + 2048 * i) for i in range(2)]
        ikb = [at(f"ikb{i}", [HD, NKEY], RING + 16384 + 4160 * i) for i in range(2)]
        iqb = at("iqb", [HD, NB, 36], RING + 24704)
        iknew = at("iknew", [HD, NB], RING + 25856)
        reld = at("reld", [32, NKEY], RING + 25920)
        qsq = at("qsq", [P, ALLT, QK], Q5 + 8192)
        junk = at("junk", [P, S_ALL], RP + 27648, BF16)
        eqb = at("eqb", [P, NKEY], RP + 29760)
        preb = at("preb", [P, NKEY], RP + 33920)
        xr = at("xr", [P, LT, NTOK + 3], Q5)
        gel = at("gel", [P, LT, NTOK], Q5 + 16576)
        kT = at("kT", [P, NKV, 2, T], RH, F32R)
        stk = at("stk", [P, NH, 2, HD], RH + 16384)
        qT = at("qT", [P, NH, P], RH + 20480, F32R)
        lg = [at(f"lg{i}", [P, T], RH + 24576 + 4096 * i) for i in range(2 * GRP)]
        pT = [at(f"pT{i}", [P, GRP * P], Q5 + 2048 * i) for i in range(4)]
        v1 = at("v1", [P, NTT, NKV, 2 * HD], RP + 27648)
        cmask = at("cmask", [P, 2 * P], RP + 35840)
        rs = at("rs", [HD, GRP * P], RP + 36864)
        lru_t = [at(f"lru{i}", [P, NTOK], RH + 43008 + 4160 * i) for i in range(4)]
        lrow = at("lrow", [80, P], RH + 59712)
        attT = at("attT", [P, ALLT, LT, P], RP)
        kpg = [at(f"kpg{i}", [P, PG, P], RING + 4096 * i) for i in range(NB)]
        vpg = [at(f"vpg{i}", [P, PG, P], Q5 + 8192 + 4096 * i if i < 2 else RH + 34816 + 4096 * (i - 2))
               for i in range(NB)]
        kbT = [at(f"kbT{i}", [P, NKEY], RH + 16384 + 4160 * i) for i in range(2)]
        qb = at("qb", [P, NB, 72], RH + 24704)
        knew = at("knew", [P, NB], RH + 27008)
        dlg = at("dlg", [64, NKEY], RH + 27072)
        dpT = at("dpT", [P, PG, 64], RH + 31232)
        ddg = at("ddg", [64, 64], RH + 33280)
        ptl = at("ptl", [NB, 64], RH + 33536)
        nsq = [at(f"nsq{i}", [P, NTOK], RP + 39328 + 4160 * i) for i in range(2)]
        nr = [at(f"nr{i}", [P, NTOK], RP + 47648 + 4160 * i) for i in range(2)]
        nt = at("nt", [P, NTOK], RP + 55968)
        mixH = at("mixH", [P, KD, NTOK], RH, F32R)
        mixL = at("mixL", [P, KD, NTOK], RH + KD * NTOK * 4, F32R)
        h2H = at("h2H", [P, KD, NTOK], RH, F32R)
        h2L = at("h2L", [P, KD, NTOK], RH + KD * NTOK * 4, F32R)
        aH = at("aH", [P, 4, NTOK], RP, F32R)
        aL = at("aL", [P, 4, NTOK], RP + 16512, F32R)
        sg = at("sg", [P, NTOK], RP + 33024)
        af = at("af", [P, NTOK], RP + 47648)
        yo = [at(f"yo{i}", [P, D], RP + 39328 + 4096 * i) for i in range(2)]

        ps = ctx.enter_context(nc.psum_tensor("ps", [P, 8, 512], F32))
        spill = nc.dram_tensor("x_feature_major", (P, KD, NTOK), F32).ap()

        def wide(b):
            return ps[:, b:b + 3, 0:CW]

        def cols(ap):
            return ap.rearrange("p (c n) -> p c n", c=NCH)

        s_const = sem("const_loaded")
        s_small = sem("small_loaded")
        s_wbd0 = sem("gate_weights_cleared")
        s_wbd = sem("gate_weights_loaded")
        s_x = [sem(f"x_loaded{i}") for i in range(NTT)]
        s_ada = [sem(f"ada_loaded{i}") for i in range(4)]
        s_modk = sem("ada_chunk_used")
        s_csi = sem("c_silu_done")
        s_tr = sem("x_transposed")
        s_xta = sem("x_evacuated_act")
        s_xtv = sem("x_evacuated_dve")
        s_mt = sem("small_transposed")
        s_mte = sem("small_evacuated")
        s_exl = sem("exp_lambda")
        s_ikst = sem("index_keys_stored")
        s_kvst = sem("keys_values_stored")
        s_sq = sem("squares_ready")
        s_squ = sem("squares_used")
        s_var = sem("variance_ready")
        s_rt = sem("root_ready")
        s_t = sem("norm_ready")
        s_h = sem("high_ready")
        s_l = sem("low_ready")
        s_spill = sem("x_spilled")
        s_craw = [sem(f"chunk_loaded{i}") for i in range(2)]
        s_cH = sem("chunk_high")
        s_cL = sem("chunk_low")
        s_pj = sem("proj_done")
        s_pja = sem("proj_evacuated_act")
        s_pjv = sem("proj_evacuated_dve")
        s_clr = sem("sample_rows_cleared")
        s_qsq = sem("qk_squares")
        s_qv = sem("qk_variance")
        s_qr = sem("qk_root")
        s_qkr = sem("qk_rotated")
        s_iqr = sem("iq_rotated")
        s_is = sem("index_high")
        s_il = sem("index_low")
        s_it = sem("index_transposed")
        s_ite = sem("index_transposed_evacuated")
        s_ikte = sem("index_keys_evacuated")
        s_sc = sem("scores_product")
        s_re = sem("scores_relu")
        s_sa = sem("scores_added")
        s_ipg = [sem(f"index_page_loaded{i}") for i in range(2)]
        s_dit = sem("decode_index_transposed")
        s_die = sem("decode_index_evacuated")
        s_dis = sem("decode_index_product")
        s_dir = sem("decode_index_relu")
        s_diw = sem("decode_iw")
        s_dsc = sem("decode_scores")
        s_thr = sem("threshold_ready")
        s_sgn = sem("signs_summed")
        s_sel = sem("selection_done")
        s_wr = [sem(f"unit_loaded{i}") for i in range(SLOTS)]
        s_wH = sem("unit_high")
        s_wL = sem("unit_low")
        s_un = sem("unit_used")
        s_lev = sem("lru_evacuated")
        s_xc = sem("conv_done")
        s_gp = sem("gate_product")
        s_gs = sem("gate_sigmoid")
        s_ga = sem("decay_ready")
        s_lu = sem("lru_root_input")
        s_lq = sem("lru_root")
        s_lh = sem("lru_tile_done")
        s_lt = sem("lasts_transposed")
        s_lte = sem("lasts_evacuated")
        s_kst = sem("k_stack")
        s_kt = sem("k_transposed")
        s_kte = sem("k_evacuated")
        s_qs = sem("q_stack_high")
        s_ql = sem("q_stack_low")
        s_v1 = sem("values_laid_out")
        s_lg = sem("logits_ready")
        s_lm = sem("logits_masked")
        s_ex = sem("probs_ready")
        s_bt = sem("bank_transposed")
        s_bte = sem("bank_evacuated")
        s_pv = sem("key_block_mixed")
        s_hd = sem("heads_placed")
        s_kpg = [sem(f"k_pages_loaded{i}") for i in range(NB)]
        s_vpg = [sem(f"v_pages_loaded{i}") for i in range(NB)]
        s_dqt = sem("decode_q_transposed")
        s_dqe = sem("decode_q_evacuated")
        s_dkt = sem("decode_keys_transposed")
        s_dke = sem("decode_keys_evacuated")
        s_dlg = sem("decode_logits")
        s_dmx = sem("decode_max")
        s_dex = sem("decode_exp")
        s_dpn = sem("decode_probs")
        s_dpt = sem("decode_probs_transposed")
        s_dpe = sem("decode_probs_evacuated")
        s_dpu = sem("decode_pages_used")
        s_dat = sem("decode_heads_placed")
        s_gsq = sem("group_squares")
        s_gsu = sem("group_squares_used")
        s_gv = sem("group_variance")
        s_gr = sem("group_root")
        s_gt = sem("group_norm")
        s_gH = sem("mix_high")
        s_gL = sem("mix_low")
        s_xback = sem("x_reloaded")
        s_res = sem("residual_added")
        s_a2 = sem("second_mod_ready")
        s_sq2 = sem("squares2_ready")
        s_su2 = sem("squares2_used")
        s_v2 = sem("variance2_ready")
        s_r2 = sem("root2_ready")
        s_t2 = sem("norm2_ready")
        s_h2 = sem("high2_ready")
        s_l2 = sem("low2_ready")
        s_sg = sem("gate_silu")
        s_af = sem("ffn_product")
        s_aH = sem("ffn_high")
        s_aL = sem("ffn_low")
        s_dn = sem("down_product")
        s_dne = sem("down_added")
        s_yt = sem("y_transposed")
        s_yea = sem("y_evacuated")
        s_y = sem("y_final")
        s_yst = [sem(f"y_stored{i}") for i in range(2)]
        s_out = sem("outputs_stored")

        w_in = a["w_in"][0]
        gate_src = a["w_gate"][0].rearrange("(k p) n -> p k n", p=P)
        up_src = a["w_up"][0].rearrange("(k p) n -> p k n", p=P)
        out_src = a["w_out"][0].rearrange("(k p) n -> p k n", p=P)
        in_src = w_in.rearrange("(k p) n -> p k n", p=P)
        ada_src = a["ada_w"][0].rearrange("(k p) n -> p k n", p=P)

        block = ctx.enter_context(nc.Block())

        @block.sync
        def _(sp):
            sp.dma_start(consts[:], a["consts"]).then_inc(s_const, 16)
            sp.dma_start(c_in[0:1, :], a["c_prompt"]).then_inc(s_small, 16)
            sp.dma_start(c_in[1:1 + NB, :], a["c_sample"]).then_inc(s_small, 16)
            sp.dma_start(xs_in[:], a["x_sample"].rearrange("b t d -> (b t) d")).then_inc(s_small, 16)
            for name, row, n in (("ln1_g", V_LN1, 8), ("ln2_g", V_LN2, 8), ("conv_b", V_CB, 4), ("lru_ba", V_BA, 4),
                                 ("lru_bx", V_BX, 4), ("lru_lambda", V_LAM, 4), ("gn_lru_g", V_GL, 4),
                                 ("gn_att_g", V_GA, 4), ("ada_b", V_ADA, 48)):
                sp.dma_start(vrows[row:row + n, :], a[name][0].rearrange("(r f) -> r f", f=P)).then_inc(s_small, 16)
            sp.dma_start(vrows[V_CW:V_CW + 16, :],
                         a["conv_w"][0].rearrange("i (c f) -> (i c) f", f=P)).then_inc(s_small, 16)
            sp.dma_start(strows[0:32, :], a["state_h"][0].rearrange("b (c f) -> (b c) f", f=P)).then_inc(s_small, 16)
            sp.dma_start(strows[32:128, :],
                         a["state_conv"][0].rearrange("b i (c f) -> (b i c) f", f=P)).then_inc(s_small, 16)
            sp.dma_start(grow[0:1, 0:HD], a["q_norm_g"]).then_inc(s_small, 16)
            sp.dma_start(grow[0:1, HD:2 * HD], a["k_norm_g"]).then_inc(s_small, 16)
            sp.dma_start(pt_sb[:], a["page_table"].rearrange("(a b) g -> a (b g)", a=1)).then_inc(s_small, 16)
            for i in range(NTT):
                sp.dma_start(xin[:, i, :], a["x_prompt"][0, i * P:(i + 1) * P, :]).then_inc(s_x[i], 16)
            for j in range(12):
                if j >= 4:
                    sp.wait_ge(s_modk, j - 3)
                sp.dma_start(ada[j % 4][:], ada_src[:, :, j * 512:(j + 1) * 512]).then_inc(s_ada[j % 4], 16)
            sp.wait_ge(s_l, KD + 1)
            sp.dma_start(spill, xT[:]).then_inc(s_spill, 16)
            for j, (c0, w) in enumerate(CHUNKS):
                if j == 0:
                    sp.wait_ge(s_modk, 12)
                    sp.wait_ge(s_mte, 3)
                if j == 2:
                    sp.wait_ge(s_cL, 1)
                sp.dma_start(craw[j % 2][:, :, 0:w], in_src[:, :, c0:c0 + w]).then_inc(s_craw[j % 2], 16)
            sp.wait_ge(s_pj, 27)
            for b in range(NB):
                if b >= 2:
                    sp.wait_ge(s_dit, b - 1)
                for g in range(PG):
                    page = sp.value_load(pt_sb[0:1, b * PG + g:b * PG + g + 1], min_val=0, max_val=NPOOL - 1)
                    sp.dma_start(ipg[b % 2][:, g, :],
                                 a["cache_ik"][0][bass.ds(page, 1), :, :].rearrange("a s d -> (a s) d")
                                 ).then_inc(s_ipg[b % 2], 16)
            sp.wait_ge(s_iqr, 1)
            sp.dma_start(o["ik_prompt"][0, 0].rearrange("(t p) d -> p t d", p=P),
                         iqk[:, 0:NTT, IH * HD:IH * HD + HD]).then_inc(s_ikst, 16)
            sp.dma_start(o["ik_sample"][0].rearrange("b t d -> (b t) d"),
                         iqk[0:NB, NTT, IH * HD:IH * HD + HD]).then_inc(s_ikst, 16)
            sp.wait_ge(s_pja, 19)
            sp.wait_ge(s_pjv, 13)
            sp.dma_start(o["v_prompt"][0, 0].rearrange("(t p) k d -> p t (k d)", p=P),
                         vt[:, 0:NTT, :]).then_inc(s_kvst, 16)
            sp.dma_start(o["v_sample"][0].rearrange("b t k d -> (b t) (k d)"), vt[0:NB, NTT, :]).then_inc(s_kvst, 16)
            sp.wait_ge(s_qkr, 1)
            sp.dma_start(o["k_prompt"][0, 0].rearrange("(t p) k d -> p t (k d)", p=P),
                         qk[:, 0:NTT, NH * HD:QK]).then_inc(s_kvst, 16)
            sp.dma_start(o["k_sample"][0].rearrange("b t k d -> (b t) (k d)"),
                         qk[0:NB, NTT, NH * HD:QK]).then_inc(s_kvst, 16)
            sp.dma_start(o["conv_sample"][0, :, 0:2, :], a["state_conv"][0, :, 1:3, :]).then_inc(s_out, 16)

            def load_unit(u, src, first=False):
                if u >= SLOTS:
                    sp.wait_ge(s_wL, u - SLOTS + 1)
                sp.dma_start(wraw[u % SLOTS][:], src).then_inc(s_wr[u % SLOTS], 16)

            sp.wait_ge(s_dsc, 1)
            sp.wait_ge(s_qkr, 1)
            for u in range(NU_LRU):
                c0 = (u // 2) * P + (u % 2) * LRU
                load_unit(u, in_src[:, :, c0:c0 + P])
            sp.wait_ge(s_lte, 1)
            sp.dma_start(o["h_prompt"][0, 0].rearrange("(c f) -> c f", f=P), lrow[0:4, :]).then_inc(s_out, 16)
            sp.dma_start(o["h_sample"][0].rearrange("b (c f) -> (b c) f", f=P), lrow[4:36, :]).then_inc(s_out, 16)
            sp.dma_start(o["conv_prompt"][0, 0].rearrange("i (c f) -> (i c) f", f=P),
                         lrow[36:48, :]).then_inc(s_out, 16)
            sp.dma_start(o["conv_sample"][0, :, 2, :].rearrange("b (c f) -> b c f", f=P),
                         lrow[48:80, :]).then_inc(s_out, 16)
            def pages(dst, name, ready, b):
                for g in range(PG):
                    page = sp.value_load(pt_sb[0:1, b * PG + g:b * PG + g + 1], min_val=0, max_val=NPOOL - 1)
                    sp.dma_start(dst[b][:, g, :],
                                 a[name][0][bass.ds(page, 1)].rearrange("a s k d -> (a s) (k d)")
                                 ).then_inc(ready[b], 16)

            sp.wait_ge(s_un, NU_LRU)
            for b in range(NB):
                pages(kpg, "cache_k", s_kpg, b)
            for b in range(2):
                pages(vpg, "cache_v", s_vpg, b)
            sp.wait_ge(s_hd, NG)
            for b in range(2, NB):
                pages(vpg, "cache_v", s_vpg, b)
            sp.wait_ge(s_dkt, NB)
            for n in range(NU_OUT):
                load_unit(U_OUT + n, out_src[:, :, n * P:(n + 1) * P])
            sp.wait_ge(s_gL, 8)
            sp.wait_ge(s_spill, 16)
            sp.dma_start(xT[:], spill).then_inc(s_xback, 16)

            def load_ffn(u, slot, k, f0, n=0):
                sp.wait_ge(s_wL, n + (u - SLOTS + 1))
                if k < 4:
                    src = (gate_src, up_src)[k % 2][:, :, bass.ds(f0 * P + (k // 2) * P, P)]
                    sp.dma_start(wraw[slot][:], src).then_inc(s_wr[slot], 16)
                else:
                    src = a["w_down"][0][bass.ds(f0 * P + (k - 4) * P, P), :]
                    sp.dma_start(wraw[slot][:].rearrange("p k n -> p (k n)"), src).then_inc(s_wr[slot], 16)

            for k in range(4):
                load_ffn(U_FFN + k, (U_FFN + k) % SLOTS, k, 0)
            with sp.Fori(0, FB // 2) as i:
                for b in range(2):
                    for k in range(UPB):
                        u = U_FFN + 4 + UPB * b + k
                        load_ffn(u, u % SLOTS, k, i * 4 + (2 + 2 * b if k < 4 else 2 * b), i * (2 * UPB))
            for k in range(4, 6):
                u = U_ALL - 6 + k
                load_ffn(u, u % SLOTS, k, FT - 2)
            for i in range(ALLT):
                sp.wait_ge(s_yea, 2 * i + 2)
                if i < NTT:
                    sp.dma_start(o["y_prompt"][0, i * P:(i + 1) * P, :], yo[i % 2][:]).then_inc(s_yst[i % 2], 16)
                else:
                    sp.dma_start(o["y_sample"].rearrange("b t d -> (b t) d"),
                                 yo[i % 2][0:NB, :]).then_inc(s_yst[i % 2], 16)
            sp.wait_ge(s_yst[0], 16 * 5)
            sp.wait_ge(s_yst[1], 16 * 4)
            sp.wait_ge(s_ikst, 16 * 2)
            sp.wait_ge(s_kvst, 16 * 4)
            sp.wait_ge(s_out, 16 * 5)

        @block.gpsimd
        def _(pool):
            pool.memset(wbd[:], 0.0).then_inc(s_wbd0, 1)
            pool.wait_ge(s_wbd0, 1)
            for gate, name in enumerate(("lru_wa", "lru_wx")):
                for h in range(2):
                    pool.dma_start(wbd[h * 64:(h + 1) * 64, gate, :, h * 64:(h + 1) * 64],
                                   a[name][0].rearrange("(c h) i j -> h i c j", h=2)[h]).then_inc(s_wbd, 16)
            for j, (c0, w) in enumerate(CHUNKS):
                pool.wait_ge(s_cH, j + 1)
                if j == 1:
                    pool.wait_ge(s_spill, 16)
                if j == 2:
                    pool.wait_ge(s_pj, 9)
                pool.tensor_tensor(cL[j % 2][:, :, 0:w], craw[j % 2][:, :, 0:w],
                                   cH[j % 2][:, :, 0:w].bitcast(F32), ALU.subtract).then_inc(s_cL, 1)

            def low(u, n=0):
                s = u % SLOTS
                pool.wait_ge(s_wH, n + (u + 1))
                pool.tensor_tensor(wL[s][:], wraw[s][:], wH[s][:].bitcast(F32), ALU.subtract).then_inc(s_wL, 1)

            for u in range(U_FFN):
                low(u)
            for u in range(U_FFN, U_FFN + 4):
                low(u)
            with pool.Fori(0, FB // 2) as i:
                for k in range(2 * UPB):
                    low(U_FFN + 4 + k, i * (2 * UPB))
            low(U_ALL - 2)
            low(U_ALL - 1)

        @block.scalar
        def _(act):
            A = nc.scalar.activation

            act.wait_ge(s_small, 16 * 18)
            A(c_si[:], c_in[:], ACT.Silu).then_inc(s_csi, 1)
            for g in range(0, 16, 2):
                act.wait_ge(s_tr, g + 1)
                i, hf = g // 2, g % 2
                nc.scalar.copy(xT[:, 4 * hf:4 * hf + 4, i * P:(i + 1) * P],
                               ps[:, g % 4, :].rearrange("p (k t) -> p k t", k=4)).then_inc(s_xta, 1)
            act.drain()
            act.wait_ge(s_xtv, 8)
            act.wait_ge(s_mte, 3)
            A(sp2[:, 0, :], sp2[:, 0, :], ACT.Exp, scale=-1.0).then_inc(s_exl, 1)
            for d in range(KD):
                if d >= 2:
                    act.wait_ge(s_squ, d - 1)
                A(sq[d % 2][:], xT[:, d, :], ACT.Square).then_inc(s_sq, 1)
            act.wait_ge(s_var, 1)
            A(rb[:], rb[:], ACT.Sqrt).then_inc(s_rt, 1)
            for d in range(KD):
                act.wait_ge(s_t, d + 1)
                A(hH[:, d, 0:T], tt[:, 0:T], ACT.Identity, bias=mod[:, d, 0:1]).then_inc(s_h, 1)
            act.wait_ge(s_t, KD + 1)
            nc.scalar.copy(hH[:, :, T:NTOK], samp[:]).then_inc(s_h, 1)

            def chunk_high(j):
                w = CHUNKS[j][1]
                act.wait_ge(s_craw[j % 2], 16 * (j // 2 + 1))
                if j == 0:
                    act.wait_ge(s_l, KD + 1)
                if j == 1:
                    act.wait_ge(s_spill, 16)
                if j == 2:
                    act.wait_ge(s_pj, 9)
                nc.scalar.copy(cH[j % 2][:, :, 0:w], craw[j % 2][:, :, 0:w]).then_inc(s_cH, 1)

            chunk_high(0)
            chunk_high(1)
            for n in range(0, 27, 2):
                j, i = n // 9, n % 9
                m = P if i < NTT else NB
                if n == 10:
                    chunk_high(2)
                if n == 0:
                    act.wait_ge(s_clr, 1)
                act.wait_ge(s_pj, n + 1)
                if j == 0:
                    nc.scalar.copy(iqk[0:m, i, :], ps[0:m, n % 6, 0:IQK]).then_inc(s_pja, 1)
                elif j == 1:
                    nc.scalar.copy(qk[0:m, i, 0:384], ps[0:m, n % 6, 0:384]).then_inc(s_pja, 1)
                else:
                    nc.scalar.copy(qk[0:m, i, 384:QK], ps[0:m, n % 6, 0:256]).then_inc(s_pja, 1)
                    nc.scalar.copy(vt[0:m, i, :], ps[0:m, n % 6, 256:384]).then_inc(s_pja, 1)
            act.drain()
            act.wait_ge(s_iqr, 1)
            for i in range(NTT):
                s = i % 2
                if i >= 2:
                    act.wait_ge(s_it, i - 1)
                nc.scalar.copy(istk[s][:, :, 0, :].bitcast(F32R),
                               iqk[:, i, 0:IH * HD].rearrange("p (h d) -> p h d", h=IH)).then_inc(s_is, 1)
                for r in range(2):
                    nc.scalar.copy(ikstk[s][:, 0, r, :].bitcast(F32R),
                                   iqk[:, i, IH * HD:IH * HD + HD]).then_inc(s_is, 1)
                act.wait_ge(s_it, i + 1)
                if i >= FIRST_SEL + 2:
                    act.wait_ge(s_sc, IH * (i - 1 - FIRST_SEL))
                nc.scalar.copy(iqT[s][:], ps[:, 4 + s, :].rearrange("p (h t) -> p h t", h=IH)).then_inc(s_ite, 1)
                nc.scalar.copy(ikT[:, :, i * P:(i + 1) * P],
                               ps[:, 6 + s, 0:256].rearrange("p (r t) -> p r t", r=2)).then_inc(s_ikte, 1)
                if i >= FIRST_SEL:
                    w = P * (i + 1)
                    for h in range(IH):
                        g = IH * (i - FIRST_SEL) + h
                        act.wait_ge(s_sc, g + 1)
                        if g >= 2:
                            act.wait_ge(s_sa, g - 1)
                        A(relu[g % 2][:, 0:w],
                          ps[:, 2 * (g % 2):2 * (g % 2) + 2, :].rearrange("p b n -> p (b n)")[:, 0:w],
                          ACT.Relu).then_inc(s_re, 1)
            act.wait_ge(s_dis, 1)
            A(reld[:, 0:1024], ps[0:32, 0:2, :].rearrange("p b n -> p (b n)"), ACT.Relu).then_inc(s_dir, 1)
            A(reld[:, 1024:1025], ps[0:32, 2, 0:1], ACT.Relu).then_inc(s_dir, 1)
            act.wait_ge(s_sa, IH * (NTT - FIRST_SEL))
            act.wait_ge(s_ikte, NTT)
            act.drain()
            A(qsq[:], qk[:], ACT.Square).then_inc(s_qsq, 1)
            act.wait_ge(s_qv, 1)
            A(rstd[:], rstd[:], ACT.Sqrt).then_inc(s_qr, 1)

            def high(u):
                s = u % SLOTS
                act.wait_ge(s_wr[s], 16 * (u // SLOTS + 1))
                if u >= SLOTS:
                    act.wait_ge(s_un, u - SLOTS + 1)
                nc.scalar.copy(wH[s][:], wraw[s][:]).then_inc(s_wH, 1)

            def signs(r):
                act.wait_ge(s_thr, r + 1)
                for n in range(SEL_ACT, NSEL):
                    i, m, w, off = SEL[n]
                    ins = A(junk[0:m, off:off + w], score[0:m, off:off + w], ACT.Sign, scale=-1.0,
                            bias=keyX[0:m, n:n + 1].bitcast(F32), accum_out=cnt[0:m, n:n + 1])
                act.drain().then_inc(s_sgn, 1)

            high(0)
            act.wait_ge(s_qkr, 1)
            bits = 0
            for u in range(NU_LRU):
                c = u // 2
                if u + 1 < NU_LRU:
                    high(u + 1)
                for _ in range(3):
                    signs(bits)
                    bits += 1
                act.wait_ge(s_un, u + 1)
                if u % 2 == 0:
                    nc.scalar.copy(cols(xr[:, c, 3:3 + NTOK]), wide(0)).then_inc(s_lev, 1)
                else:
                    A(cols(gel[:, c, :]), wide(3), ACT.Gelu_apprx_tanh).then_inc(s_lev, 1)
            for r in range(bits, KEY_BITS):
                signs(r)
            for c in range(LT):
                xc, ga, gg, gt = lru_t
                act.wait_ge(s_gp, c + 1)
                if c >= 1:
                    act.wait_ge(s_lh, c)
                A(cols(ga[:]), wide(0), ACT.Sigmoid, bias=vec[:, V_BA + c:V_BA + c + 1]).then_inc(s_gs, 1)
                A(cols(gg[:]), wide(3), ACT.Sigmoid, bias=vec[:, V_BX + c:V_BX + c + 1]).then_inc(s_gs, 1)
                act.drain()
                A(gt[:], ga[:], ACT.Tanh, scale=nsp[:, 1, c:c + 1]).then_inc(s_ga, 1)
                act.drain()
                A(ga[:], ga[:], ACT.Exp, scale=nsp[:, 0, c:c + 1]).then_inc(s_ga, 1)
                act.wait_ge(s_lu, c + 1)
                A(gt[:], gt[:], ACT.Sqrt).then_inc(s_lq, 1)
            for i in range(NTT):
                act.wait_ge(s_kst, i + 1)
                act.wait_ge(s_kt, i + 1)
                nc.scalar.copy(kT[:, :, :, i * P:(i + 1) * P],
                               ps[:, 6 + i % 2, :].rearrange("p (k r t) -> p k r t", k=NKV, r=2)).then_inc(s_kte, 1)

            def q_high(i):
                if i == 0:
                    act.wait_ge(s_kt, NTT)
                else:
                    act.wait_ge(s_bt, q_item(2 * i - 1) + 1)
                nc.scalar.copy(stk[:, :, 0, :].bitcast(F32R),
                               qk[:, i, 0:NH * HD].rearrange("p (h d) -> p h d", h=NH)).then_inc(s_qs, 1)

            def q_evac(n):
                act.wait_ge(s_bt, q_item(n) + 1)
                if n >= 2:
                    act.wait_ge(s_lg, GRP * (n - 1))
                nc.scalar.copy(qT[:, GRP * (n % 2):GRP * (n % 2 + 1), :],
                               ps[:, 4 + q_item(n) % 2, :].rearrange("p (h t) -> p h t", h=GRP)).then_inc(s_bte, 1)

            def exponential(g):
                n = g // GRP
                act.wait_ge(s_lm, g + 1)
                buf = lg[g % 8][:, 0:P * (tile_of(n) + 1)]
                A(buf, buf, ACT.Exp, bias=nb[:, g % 8:g % 8 + 1], scale=-1.0).then_inc(s_ex, 1)

            q_high(0)
            q_evac(0)
            for h in range(GRP):
                exponential(h)
            for n in range(NG):
                i = tile_of(n)
                if n + 1 < NG:
                    q_evac(n + 1)
                for step in range(max(GRP, i + 1)):
                    if step <= i:
                        item, kb = first_item(n) + step, key_count(n) + step
                        act.wait_ge(s_bt, item + 1)
                        if kb >= 4:
                            act.wait_ge(s_pv, kb - 3)
                        nc.scalar.copy(pT[kb % 4][:], ps[:, 4 + item % 2, :]).then_inc(s_bte, 1)
                    if n + 1 < NG and step < GRP:
                        exponential(GRP * (n + 1) + step)
                if n % 2 == 0 and i + 1 < NTT:
                    q_high(i + 1)
            for b in range(NB):
                act.wait_ge(s_dkt, b + 1)
                if b >= 2:
                    act.wait_ge(s_dlg, b)
                s = b % 2
                nc.scalar.copy(kbT[s][:, 0:1024], ps[:, 4:6, :].rearrange("p b n -> p (b n)")).then_inc(s_dke, 1)
                if b == 0:
                    act.wait_ge(s_dqe, 2)
                nc.scalar.copy(kbT[s][:, 1024:1025], knew[:, b:b + 1]).then_inc(s_dke, 1)
            act.wait_ge(s_dmx, 1)
            A(dlg[:], dlg[:], ACT.Exp, bias=dsm[:, 1:2], scale=SCALE, accum_out=dsm[:, 2:3]).then_inc(s_dex, 1)
            for n in range(8):
                if n >= 2:
                    act.wait_ge(s_gsu, n - 1)
                c = n % 4
                if n < 4:
                    if n == 0:
                        act.wait_ge(s_dat, 4)
                    A(nsq[n % 2][:], gel[:, c, :], ACT.Square).then_inc(s_gsq, 2)
                else:
                    A(nsq[n % 2][:, 0:T].rearrange("p (t n) -> p t n", t=NTT), attT[:, 0:NTT, c, :],
                      ACT.Square).then_inc(s_gsq, 1)
                    A(nsq[n % 2][:, T:NTOK], attT[:, NTT, c, 0:NB], ACT.Square).then_inc(s_gsq, 1)
            for u in range(U_OUT, U_OUT + 3):
                high(u)
            act.wait_ge(s_gv, 2)
            A(nr[0][:], nr[0][:], ACT.Sqrt).then_inc(s_gr, 1)
            A(nr[1][:], nr[1][:], ACT.Sqrt).then_inc(s_gr, 1)
            act.wait_ge(s_out, 16 * 5)
            for n in range(8):
                act.wait_ge(s_gt, n + 1)
                nc.scalar.copy(mixH[:, n, :], nt[:]).then_inc(s_gH, 1)
            for u in range(U_OUT + 3, U_FFN):
                high(u)
            for d in range(KD):
                if d == 0:
                    act.wait_ge(s_res, KD + 1)
                if d >= 2:
                    act.wait_ge(s_su2, d - 1)
                A(nsq[d % 2][:], xT[:, d, :], ACT.Square).then_inc(s_sq2, 1)
            act.wait_ge(s_v2, 1)
            A(nr[0][:], nr[0][:], ACT.Sqrt).then_inc(s_r2, 1)
            for d in range(KD):
                act.wait_ge(s_t2, d + 1)
                A(h2H[:, d, 0:T], nt[:, 0:T], ACT.Identity, bias=mod[:, 24 + d, 0:1]).then_inc(s_h2, 1)
            act.wait_ge(s_t2, KD + 1)
            nc.scalar.copy(h2H[:, :, T:NTOK], samp[:]).then_inc(s_h2, 1)

            def split(u, i=None):
                s = u % SLOTS
                act.wait_ge(s_wr[s], (i * 64 if i is not None else 0) + 16 * (u // SLOTS + 1))
                nc.scalar.copy(wH[s][:], wraw[s][:]).then_inc(s_wH, 1)

            def slot_free(k, b, i=None):
                n4 = i * 8 if i is not None else 0
                n24 = i * 48 if i is not None else 0
                act.wait_ge(s_un, n4 + (U_FFN + 4 * b + (0, 0, 0, 1, 2, 3)[k]))
                if k in (1, 2):
                    act.wait_ge(s_dn, n24 + (24 * (b - 1) + 1))

            def gate_act(f, par, b, i=None):
                n2 = i * 4 if i is not None else 0
                n4 = i * 8 if i is not None else 0
                act.wait_ge(s_un, n4 + (U_FFN + 4 * b + 2 * f + 1))
                act.wait_ge(s_af, n2 + (2 * b + f + 1))
                A(cols(sg[:]), wide(0), ACT.Silu).then_inc(s_sg, 1)

            def product_high(f, par, b, i=None):
                n2 = i * 4 if i is not None else 0
                act.wait_ge(s_af, n2 + (2 * b + f + 2))
                nc.scalar.copy(aH[:, 2 * par + f, :], af[:]).then_inc(s_aH, 1)

            act.drain().then_inc(s_sg, 1)
            high(U_FFN)
            high(U_FFN + 1)
            high(U_FFN + 2)
            gate_act(0, 0, 0)
            high(U_FFN + 3)
            product_high(0, 0, 0)
            gate_act(1, 0, 0)
            product_high(1, 0, 0)
            slot_free(0, 1)
            split(U_FFN + 4)
            with act.Fori(0, FB // 2) as i:
                for q in range(2):
                    b, par, u = 1 + q, (1 + q) % 2, U_FFN + 4 + UPB * q
                    for k in (1, 2):
                        slot_free(k, b, i)
                        split(u + k, i)
                    gate_act(0, par, b, i)
                    slot_free(3, b, i)
                    split(u + 3, i)
                    product_high(0, par, b, i)
                    slot_free(4, b, i)
                    split(u + 4, i)
                    gate_act(1, par, b, i)
                    slot_free(5, b, i)
                    split(u + 5, i)
                    product_high(1, par, b, i)
                    slot_free(0, b + 1, i)
                    split(u + 6, i)
            act.wait_ge(s_dn, 24 * (FB - 1) + 1)
            split(U_ALL - 1)

            for i in range(ALLT):
                m = P if i < NTT else NB
                act.wait_ge(s_yt, 2 * i + 1)
                if i >= 2:
                    act.wait_ge(s_yst[i % 2], 16 * (i // 2))
                nc.scalar.copy(yo[i % 2][0:m, 0:512], ps[0:m, 2 * (i % 2), :]).then_inc(s_yea, 1)
                act.wait_ge(s_yt, 2 * i + 2)
                nc.scalar.copy(yo[i % 2][0:m, 512:D], ps[0:m, 2 * (i % 2) + 1, :]).then_inc(s_yea, 1)

        @block.vector
        def _(dve):
            V = nc.vector

            def stt(out, in0, scalar, in1, op0, op1):
                return V.scalar_tensor_tensor(out=out, in0=in0, scalar=scalar, in1=in1, op0=op0, op1=op1)

            for g in range(1, 16, 2):
                dve.wait_ge(s_tr, g + 1)
                i, hf = g // 2, g % 2
                V.tensor_copy(xT[:, 4 * hf:4 * hf + 4, i * P:(i + 1) * P],
                              ps[:, g % 4, :].rearrange("p (k t) -> p k t", k=4)).then_inc(s_xtv, 1)
            dve.wait_ge(s_mt, 1)
            V.tensor_copy(xT[:, :, T:NTOK], ps[:, 4, 0:64].rearrange("p (k b) -> p k b", k=KD)).then_inc(s_mte, 1)
            dve.wait_ge(s_mt, 2)
            V.tensor_copy(cT[:], ps[:, 7, 0:72].rearrange("p (k b) -> p k b", k=KD)).then_inc(s_mte, 1)
            dve.wait_ge(s_mt, 3)
            V.tensor_copy(vec[:], ps[:, 5, 0:V_ALL])
            V.tensor_copy(stT[:], ps[:, 5, 128:256])
            V.tensor_copy(gqk[:], ps[:, 5, 256:384].rearrange("p (g d) -> p g d", g=2))
            dve.drain()
            lam = vec[:, V_LAM:V_LAM + LT]
            stt(sp2[:, 0, :], lam, -1.0, lam, ALU.mult, ALU.max).then_inc(s_mte, 1)
            dve.wait_ge(s_modk, 12)
            V.tensor_tensor(mod[:], ps[:, 6, 0:432].rearrange("p (g b) -> p g b", b=1 + NB),
                            vec[:, V_ADA:V_ADA + 48].unsqueeze(2).to_broadcast([P, 48, 1 + NB]), ALU.add)
            dve.drain()

            def gains(row, scale_at):
                V.tensor_scalar(g1p[:], mod[:, scale_at:scale_at + KD, :], 1.0, None, ALU.add)
                dve.drain()
                V.tensor_tensor(g1p[:], g1p[:], vec[:, row:row + KD].unsqueeze(2).to_broadcast([P, KD, 1 + NB]),
                                ALU.mult)
                dve.drain()

            gains(V_LN1, 8)
            dve.wait_ge(s_squ, KD)

            def variance(dst, banks, n):
                V.tensor_scalar(cols(dst), wide(banks), 1.0 / n, EPS, ALU.mult, ALU.add)

            variance(rb[:], 0, D)
            dve.drain().then_inc(s_var, 1)
            dve.wait_ge(s_rt, 1)

            def modulated(rr, t, high_t, low_t, shift_at, s_t, s_h, s_l):
                V.reciprocal(rr[:], rr[:])
                dve.drain()
                for d in range(KD):
                    stt(t[:, 0:T], xT[:, d, 0:T], g1p[:, d, 0:1], rr[:, 0:T], ALU.mult, ALU.mult).then_inc(s_t, 1)
                    dve.wait_ge(s_h, d + 1)
                    stt(low_t[:, d, 0:T], t[:, 0:T], mod[:, shift_at + d, 0:1], high_t[:, d, 0:T].bitcast(F32),
                        ALU.add, ALU.subtract).then_inc(s_l, 1)
                    dve.drain()
                V.tensor_tensor(samp[:], xT[:, :, T:NTOK], g1p[:, :, 1:], ALU.mult)
                dve.drain()
                V.tensor_tensor(samp[:], samp[:], rr[:, T:NTOK].unsqueeze(1).to_broadcast([P, KD, NB]), ALU.mult)
                dve.drain()
                V.tensor_tensor(samp[:], samp[:], mod[:, shift_at:shift_at + KD, 1:], ALU.add).then_inc(s_t, 1)
                dve.wait_ge(s_h, KD + 1)
                V.tensor_tensor(low_t[:, :, T:NTOK], samp[:], high_t[:, :, T:NTOK].bitcast(F32),
                                ALU.subtract).then_inc(s_l, 1)

            modulated(rb, tt, hH, hL, 0, s_t, s_h, s_l)
            dve.drain()
            dve.wait_ge(s_modk, 12)
            V.memset(qk[:, NTT, :], 0.0)
            V.memset(iqk[:, NTT, :], 0.0)
            V.memset(vt[:, NTT, :], 0.0)
            dve.drain()
            V.memset(cnt[:], 0.0).then_inc(s_clr, 1)
            for n in range(1, 27, 2):
                j, i = n // 9, n % 9
                m = P if i < NTT else NB
                dve.wait_ge(s_pj, n + 1)
                if j == 0:
                    V.tensor_copy(iqk[0:m, i, :], ps[0:m, n % 6, 0:IQK]).then_inc(s_pjv, 1)
                elif j == 1:
                    V.tensor_copy(qk[0:m, i, 0:384], ps[0:m, n % 6, 0:384]).then_inc(s_pjv, 1)
                else:
                    V.tensor_copy(qk[0:m, i, 384:QK], ps[0:m, n % 6, 0:256])
                    dve.drain()
                    V.tensor_copy(vt[0:m, i, :], ps[0:m, n % 6, 256:384]).then_inc(s_pjv, 1)
            dve.drain()
            dve.wait_ge(s_pja, 19)

            rope = consts[:, C_ROPE:C_ALL].rearrange("p (t r) -> p t r", t=ALLT)

            def rotate(buf, c0, heads):
                v = buf[:, :, c0:c0 + heads * HD].rearrange("p t (h d) -> p t h d", h=heads)
                x1, x2 = v[:, :, :, 0:HALF], v[:, :, :, HALF:2 * HALF]
                cs = rope[:, :, 0:HALF].unsqueeze(2).to_broadcast([P, ALLT, heads, HALF])
                sn = rope[:, :, HALF:].unsqueeze(2).to_broadcast([P, ALLT, heads, HALF])
                t = [rt5[:, n, 0:ALLT * heads * HALF].rearrange("p (t h d) -> p t h d", t=ALLT, h=heads)
                     for n in range(4)]
                V.tensor_tensor(t[0], x1, cs, ALU.mult)
                V.tensor_tensor(t[1], x2, sn, ALU.mult)
                V.tensor_tensor(t[2], x2, cs, ALU.mult)
                V.tensor_tensor(t[3], x1, sn, ALU.mult)
                dve.drain()
                V.tensor_tensor(x1, t[0], t[1], ALU.subtract)
                last = V.tensor_tensor(x2, t[2], t[3], ALU.add)
                dve.drain()
                return last

            dve.wait_ge(s_pj, 27)
            rotate(iqk, 0, IH + 1)
            dve.drain().then_inc(s_iqr, 1)
            for i in range(NTT):
                s = i % 2
                dve.wait_ge(s_is, 3 * (i + 1))
                V.tensor_tensor(istk[s][:, :, 1, :].bitcast(F32R),
                                iqk[:, i, 0:IH * HD].rearrange("p (h d) -> p h d", h=IH), istk[s][:, :, 0, :],
                                ALU.subtract).then_inc(s_il, 1)
                V.tensor_tensor(ikstk[s][:, 1, :, :].bitcast(F32R),
                                iqk[:, i, IH * HD:IH * HD + HD].unsqueeze(1).to_broadcast([P, 2, HD]),
                                ikstk[s][:, 0, :, :], ALU.subtract).then_inc(s_il, 1)
                if i >= FIRST_SEL:
                    w = P * (i + 1)
                    sc = score[:, S_OFF[i]:S_OFF[i] + w]
                    for h in range(IH):
                        g = IH * (i - FIRST_SEL) + h
                        iw = iqk[:, i, IH * HD + HD + h:IH * HD + HD + h + 1]
                        dve.wait_ge(s_re, g + 1)
                        if h == 0:
                            V.tensor_scalar(sc, relu[g % 2][:, 0:w], iw, None, ALU.mult).then_inc(s_sa, 1)
                        else:
                            stt(sc, relu[g % 2][:, 0:w], iw, sc, ALU.mult, ALU.add).then_inc(s_sa, 1)
                        dve.drain()
                    V.tensor_tensor(sc[:, w - P:w], sc[:, w - P:w], caus, ALU.add)
                    dve.drain()
            V.memset(iqb[:], 0.0)
            dve.drain()
            dve.wait_ge(s_diw, 1)
            V.tensor_copy(iqb[:, :, 0:IH], ps[0:HD, 7, 0:32].rearrange("p (h b) -> p b h", h=IH))
            V.tensor_copy(iknew[:], ps[0:HD, 7, 32:40])
            V.tensor_tensor(iwc[:, 0:4], ps[0:32, 7, 64:68], consts[0:32, C_M4:C_M4 + 4], ALU.mult)
            dve.drain()
            V.tensor_reduce(iwc[:, 4:5], iwc[:, 0:4], AX.X, ALU.add)
            dve.drain()
            V.tensor_scalar(iwb[:], consts[0:32, C_E4T:C_E4T + 8], iwc[:, 4:5], None, ALU.mult).then_inc(s_diw, 1)
            for b in range(NB):
                dve.wait_ge(s_dit, b + 1)
                V.tensor_copy(ikb[b % 2][:, 0:1024],
                              ps[0:HD, 4:6, :].rearrange("p b n -> p (b n)")).then_inc(s_die, 1)
                V.tensor_copy(ikb[b % 2][:, 1024:1025], iknew[:, b:b + 1]).then_inc(s_die, 1)
            dve.wait_ge(s_dsc, 1)
            V.tensor_copy(score[0:NB, S_DEC:S_DEC + 1024], ps[0:NB, 4:6, :].rearrange("p b n -> p (b n)"))
            V.tensor_copy(score[0:NB, S_DEC + 1024:S_DEC + 1025], ps[0:NB, 6, 0:1])
            dve.wait_ge(s_qsq, 1)
            V.tensor_reduce(rstd[:], qsq[:].rearrange("p t (h d) -> p t h d", h=NH + NKV), AX.X, ALU.add)
            dve.drain()
            V.tensor_scalar(rstd[:], rstd[:], 1.0 / HD, EPS, ALU.mult, ALU.add).then_inc(s_qv, 1)
            dve.wait_ge(s_qr, 1)
            V.reciprocal(rstd[:], rstd[:])
            dve.drain()
            for i in range(ALLT):
                v = qk[:, i, :].rearrange("p (h d) -> p h d", h=NH + NKV)
                V.tensor_tensor(v, v, rstd[:, i, :].unsqueeze(2).to_broadcast([P, NH + NKV, HD]), ALU.mult)
            dve.drain()
            for i in range(ALLT):
                v = qk[:, i, :].rearrange("p (h d) -> p h d", h=NH + NKV)
                for g, (h0, h1) in enumerate(((0, NH), (NH, NH + NKV))):
                    V.tensor_tensor(v[:, h0:h1, :], v[:, h0:h1, :],
                                    gqk[:, g, :].unsqueeze(1).to_broadcast([P, h1 - h0, HD]), ALU.mult)
            dve.drain()
            rotate(qk, 0, NH + NKV)
            V.memset(keyK[:], 0)
            V.memset(keyX[:], 0)
            V.memset(keyC[:], -2147483648)
            V.memset(bit[:], 0x40000000)
            dve.drain().then_inc(s_qkr, 1)

            def count(op, thr, n0=0, n1=NSEL):
                for n in range(n0, n1):
                    i, m, w, off = SEL[n]
                    V.tensor_scalar(junk[0:m, off:off + w], score[0:m, off:off + w], thr[0:m, n:n + 1].bitcast(F32), 0.0,
                                    op, ALU.add, accum_out=cnt[0:m, n:n + 1])

            def take():
                V.tensor_scalar(keep[:, 0:SEL_ACT], cnt[:, 0:SEL_ACT], float(TOPK), None, ALU.is_ge)
                V.tensor_tensor(keep[:, SEL_ACT:], limit[:, SEL_ACT:], cnt[:, SEL_ACT:], ALU.is_ge)
                dve.drain()
                V.copy_predicated(keyK[:], keep[:], keyC[:])
                dve.drain()

            def top_mask(key):
                V.tensor_scalar(keyM[:], key[:], 31, None, ALU.arith_shift_right)
                dve.drain()
                V.tensor_scalar(keyM[:], keyM[:], -1, -2147483648, ALU.bitwise_xor, ALU.bitwise_or)
                dve.drain()

            for n in range(SEL_ACT, NSEL):
                V.memset(limit[:, n:n + 1], float(SEL[n][2] - 2 * TOPK + 1))
            dve.wait_ge(s_ikst, 32)
            dve.drain().then_inc(s_thr, 1)
            count(ALU.is_ge, keyX, 0, SEL_ACT)
            dve.drain()
            dve.wait_ge(s_sgn, 1)
            take()
            top_mask(keyK)
            with dve.Fori(0, KEY_BITS - 1) as bit_no:
                V.tensor_scalar(keyC[:], keyK[:], bit[:, 0:1], None, ALU.bitwise_or)
                stt(keyX[:], keyK[:], bit[:, 0:1], keyM[:], ALU.bitwise_or, ALU.bitwise_xor)
                dve.drain().then_inc(s_thr, 1)
                V.tensor_scalar(bit[:], bit[:], 1, None, ALU.logical_shift_right)
                count(ALU.is_ge, keyX, 0, SEL_ACT)
                dve.drain()
                dve.wait_ge(s_sgn, bit_no + 2)
                take()
            V.tensor_scalar(keyL[:, 0, :], keyK[:], 65535, None, ALU.bitwise_and)
            V.tensor_scalar(keyL[:, 1, :], keyK[:], 16, None, ALU.arith_shift_right)
            dve.drain()
            V.tensor_scalar(keyL[:, 0, :], keyL[:, 0, :], 1, None, ALU.add)
            dve.drain()
            V.tensor_scalar(keyN[:], keyL[:, 0, :], 16, None, ALU.arith_shift_right)
            dve.drain()
            V.tensor_tensor(keyL[:, 1, :], keyL[:, 1, :], keyN[:], ALU.add)
            V.tensor_scalar(keyL[:, 0, :], keyL[:, 0, :], 65535, None, ALU.bitwise_and)
            dve.drain()
            V.tensor_scalar(keyL[:, 1, :], keyL[:, 1, :], 16, None, ALU.logical_shift_left)
            dve.drain()
            V.tensor_tensor(keyC[:], keyL[:, 1, :], keyL[:, 0, :], ALU.bitwise_or)
            dve.drain()
            top_mask(keyC)
            V.tensor_tensor(keyX[:], keyC[:], keyM[:], ALU.bitwise_xor)
            dve.drain()
            count(ALU.is_ge, keyX, SEL_ACT)
            dve.drain()
            V.tensor_scalar(keep[:, SEL_ACT:], cnt[:, SEL_ACT:], float(TOPK), None, ALU.is_ge)
            dve.drain()
            V.copy_predicated(keyK[:, SEL_ACT:], keep[:, SEL_ACT:], keyC[:, SEL_ACT:])
            dve.drain()
            top_mask(keyK)
            V.tensor_tensor(keyX[:], keyK[:], keyM[:], ALU.bitwise_xor)
            dve.drain()
            V.tensor_scalar(keyN[:], keyX[:], 0x7FFFFFFF, None, ALU.bitwise_and)
            V.memset(keyC[:], 0)
            dve.drain()
            V.tensor_scalar(keep[:], keyN[:], float(1 << 23), None, ALU.is_lt)
            dve.drain()
            V.copy_predicated(keyX[:], keep[:], keyC[:])
            dve.drain()
            count(ALU.is_gt, keyX)
            dve.drain()
            V.tensor_scalar(cnt[:], cnt[:], -1.0, float(TOPK), ALU.mult, ALU.add)
            dve.drain()
            for n, (i, m, w, off) in enumerate(SEL):
                thr = keyX[0:m, n:n + 1].bitcast(F32)
                sc = score[0:m, off:off + w]
                e, p = eqb[0:m, 0:w], preb[0:m, 0:w]
                V.tensor_scalar(e, sc, thr, None, ALU.is_equal)
                dve.drain()
                V.tensor_tensor_scan(p, e, e, 0.0, ALU.add, ALU.max)
                dve.drain()
                stt(e, p, cnt[0:m, n:n + 1], e, ALU.is_le, ALU.mult)
                dve.drain()
                stt(p, sc, thr, e, ALU.is_gt, ALU.add)
                dve.drain()
                V.tensor_scalar(sc, p, 1.0, -NEG, ALU.subtract, ALU.mult)
                dve.drain().then_inc(s_sel, 1)

            xc, ga, gg, gt = lru_t
            e_, z_, acc_ = sp2[:, 0, :], sp2[:, 1, :], sp2[:, 2, :]
            dve.wait_ge(s_exl, 1)
            V.tensor_scalar(z_, e_, 2.0, None, ALU.add)
            dve.drain()
            V.reciprocal(z_, z_)
            dve.drain()
            V.tensor_tensor(z_, z_, e_, ALU.mult)
            dve.drain()
            z2 = nsp[:, 2, :]
            V.tensor_tensor(z2, z_, z_, ALU.mult)
            V.memset(acc_, 1.0 / 19)
            dve.drain()
            for k in range(17, 0, -2):
                V.tensor_tensor(acc_, acc_, z2, ALU.mult)
                dve.drain()
                V.tensor_scalar(acc_, acc_, 1.0 / k, None, ALU.add)
                dve.drain()
            V.tensor_tensor(acc_, acc_, z_, ALU.mult)
            V.tensor_scalar(nsp[:, 3, :], lam, -1.0, 0.0, ALU.mult, ALU.max)
            dve.drain()
            stt(acc_, acc_, 2.0, nsp[:, 3, :], ALU.mult, ALU.add)
            dve.drain()
            V.tensor_scalar(nsp[:, 0, :], acc_, -C_LRU, None, ALU.mult)
            V.tensor_scalar(nsp[:, 1, :], acc_, C_LRU, None, ALU.mult)
            dve.drain()
            dve.wait_ge(s_lev, NU_LRU)
            V.memset(xr[:, :, 0:3], 0.0)
            dve.drain()
            for c in range(LT):
                cw = [vec[:, V_CW + 4 * i + c:V_CW + 4 * i + c + 1] for i in range(4)]
                cb = vec[:, V_CB + c:V_CB + c + 1]
                cst = stT[:, 32:128].rearrange("p (b i c) -> p b i c", b=NB, i=3)
                V.tensor_scalar(xc[:, 0:T], xr[:, c, 0:T], cw[0], cb, ALU.mult, ALU.add)
                V.tensor_scalar(xc[:, T:NTOK], cst[:, :, 0, c], cw[0], cb, ALU.mult, ALU.add)
                dve.drain()
                for i in range(1, 4):
                    last = stt(xc[:, 0:T], xr[:, c, i:i + T], cw[i], xc[:, 0:T], ALU.mult, ALU.add)
                    new = cst[:, :, i, c] if i < 3 else xr[:, c, 3 + T:3 + NTOK]
                    last = stt(xc[:, T:NTOK], new, cw[i], xc[:, T:NTOK], ALU.mult, ALU.add)
                    dve.drain()
                V.tensor_copy(lasts[:, 36 + c:48:4], xr[:, c, T:T + 3])
                V.tensor_copy(lasts[:, 48 + c:80:4], xr[:, c, 3 + T:3 + NTOK])
                dve.drain().then_inc(s_xc, 1)
                dve.wait_ge(s_ga, 2 * (c + 1))
                h = xr[:, c, 3:3 + NTOK]
                V.tensor_tensor(h, ga[:], ga[:], ALU.mult)
                dve.drain()
                stt(gt[:], h, 1.0, gt[:], ALU.add, ALU.mult).then_inc(s_lu, 1)
                V.tensor_tensor(gg[:], gg[:], xc[:], ALU.mult)
                dve.wait_ge(s_lq, c + 1)
                dve.drain()
                V.tensor_tensor(gg[:], gg[:], gt[:], ALU.mult)
                dve.drain()
                V.tensor_tensor_scan(h[:, 0:T], ga[:, 0:T], gg[:, 0:T], 0.0, ALU.mult, ALU.add)
                V.tensor_tensor(h[:, T:NTOK], ga[:, T:NTOK], stT[:, c:32:4], ALU.mult)
                dve.drain()
                V.tensor_tensor(h[:, T:NTOK], h[:, T:NTOK], gg[:, T:NTOK], ALU.add)
                dve.drain()
                V.tensor_copy(lasts[:, c:c + 1], h[:, T - 1:T])
                V.tensor_copy(lasts[:, 4 + c:36:4], h[:, T:NTOK])
                V.tensor_tensor(gel[:, c, :], gel[:, c, :], h, ALU.mult)
                dve.drain().then_inc(s_lh, 1)

            dve.wait_ge(s_lt, 1)
            V.tensor_copy(lrow[:], ps[0:80, 3, 0:P]).then_inc(s_lte, 1)

            V.tensor_copy(v1[:, :, :, 0:HD], vt[:, 0:NTT, :].rearrange("p t (k d) -> p t k d", k=NKV))
            V.memset(v1[:, :, :, HD:], 1.0)
            V.memset(cmask[:, 0:P], 0.0)
            V.tensor_copy(cmask[:, P:2 * P], caus)
            dve.drain().then_inc(s_v1, 1)

            kst = stk[:].rearrange("p h r d -> p (h r d)").rearrange("p (s k r c d) -> p s k r c d", s=2, k=NKV, r=2, c=2)
            for i in range(NTT):
                s = i % 2
                if i >= 2:
                    dve.wait_ge(s_kt, i - 1)
                for k in range(NKV):
                    kv = qk[:, i, (NH + k) * HD:(NH + k + 1) * HD].unsqueeze(1).to_broadcast([P, 2, HD])
                    V.tensor_copy(kst[:, s, k, 0].bitcast(F32R), kv)
                dve.drain()
                for k in range(NKV):
                    kv = qk[:, i, (NH + k) * HD:(NH + k + 1) * HD].unsqueeze(1).to_broadcast([P, 2, HD])
                    V.tensor_tensor(kst[:, s, k, 1].bitcast(F32R), kv, kst[:, s, k, 0], ALU.subtract)
                dve.drain().then_inc(s_kst, 1)

            def q_low(i):
                dve.wait_ge(s_qs, i + 1)
                V.tensor_tensor(stk[:, :, 1, :].bitcast(F32R),
                                qk[:, i, 0:NH * HD].rearrange("p (h d) -> p h d", h=NH), stk[:, :, 0, :],
                                ALU.subtract).then_inc(s_ql, 1)

            def masked(g):
                n = g // GRP
                i = tile_of(n)
                w = P * (i + 1)
                dve.wait_ge(s_lg, g + 1)
                if n >= 2:
                    dve.wait_ge(s_bt, first_item(n - 2) + tile_of(n - 2) + 1)
                bias = score[:, S_OFF[i]:S_OFF[i] + w] if i >= FIRST_SEL else cmask[:, 2 * P - w:]
                src = ps[:, 2 * (g % 2):2 * (g % 2) + 2, :].rearrange("p b n -> p (b n)")[:, 0:w]
                V.tensor_tensor_reduce(lg[g % 8][:, 0:w], src, bias, -SCALE, 3.0e38, ALU.add, ALU.min,
                                       accum_out=nb[:, g % 8:g % 8 + 1]).then_inc(s_lm, 1)

            def place(n):
                i, kv = n // NKV, n % NKV
                dve.wait_ge(s_pv, key_count(n + 1))
                V.reciprocal(rs[:], ps[HD:P, 6 + n % 2, :])
                dve.drain()
                o3 = ps[0:HD, 6 + n % 2, :].rearrange("p (c r t) -> p r c t", c=2, r=2)
                r3 = rs[:].rearrange("p (c r t) -> p r c t", c=2, r=2)
                for par in range(2):
                    V.tensor_tensor(attT[par * HD:(par + 1) * HD, i, 2 * kv:2 * kv + 2, :], o3[:, par], r3[:, par],
                                    ALU.mult)
                dve.drain().then_inc(s_hd, 1)

            q_low(0)
            for h in range(GRP):
                masked(h)
            dve.wait_ge(s_kvst, 64)
            for n in range(NG):
                if n + 1 < NG:
                    for step in range(GRP):
                        masked(GRP * (n + 1) + step)
                        if step == 1 and n >= 1:
                            place(n - 1)
                else:
                    place(n - 1)
                if n % 2 == 0 and tile_of(n) + 1 < NTT:
                    q_low(tile_of(n) + 1)
            place(NG - 1)

            V.memset(qb[:], 0.0)
            dve.drain()
            dve.wait_ge(s_dqt, 1)
            dq = ps[:, 7, 0:32].rearrange("p (c b) -> p c b", c=4)
            for c in range(4):
                for par in range(2):
                    h, kv = 2 * c + par, c // 2
                    V.tensor_copy(qb[kv * 64:(kv + 1) * 64, :, h], dq[par * 64:(par + 1) * 64, c, :])
            dve.drain().then_inc(s_dqe, 1)
            V.tensor_copy(knew[:], ps[:, 7, 32:40]).then_inc(s_dqe, 1)
            dve.wait_ge(s_dlg, NB + 1)
            V.tensor_copy(dlg[:, 0:1024], ps[0:64, 0:2, :].rearrange("p b n -> p (b n)"))
            V.tensor_copy(dlg[:, 1024:1025], ps[0:64, 2, 0:1])
            dve.drain()
            V.tensor_reduce(dsm[:, 0:1], dlg[:], AX.X, ALU.max)
            dve.drain()
            V.tensor_scalar(dsm[:, 1:2], dsm[:, 0:1], -SCALE, None, ALU.mult).then_inc(s_dmx, 1)
            dve.wait_ge(s_dex, 1)
            V.reciprocal(dsm[:, 3:4], dsm[:, 2:3])
            dve.drain()
            V.tensor_scalar(dlg[:], dlg[:], dsm[:, 3:4], None, ALU.mult)
            dve.drain()
            V.tensor_scalar(ddg[:], consts[0:64, C_ID:C_ID + 64], dlg[:, 1024:1025], None, ALU.mult)
            dve.drain().then_inc(s_dpn, 1)
            dve.wait_ge(s_dpt, 1)
            V.tensor_copy(dpT[:], ps[:, 3, :].rearrange("p (g r) -> p g r", g=PG))
            V.tensor_copy(ptl[:], ps[0:NB, 4, 0:64])
            dve.drain().then_inc(s_dpe, 1)
            dve.wait_ge(s_dpu, NB)
            for kv in range(NKV):
                for par in range(2):
                    src = ps[kv * 64:(kv + 1) * 64, 5, 0:64].rearrange("p (b k c r) -> p k r c b", b=NB, k=NKV, c=2)
                    V.tensor_copy(attT[par * 64:(par + 1) * 64, NTT, 2 * kv:2 * kv + 2, 0:NB],
                                  src[:, kv, par]).then_inc(s_dat, 1)

            dve.wait_ge(s_gsu, 8)
            variance(nr[0][:], 0, LRU)
            variance(nr[1][:], 3, LRU)
            dve.drain().then_inc(s_gv, 2)
            dve.wait_ge(s_gr, 2)
            V.reciprocal(nr[0][:], nr[0][:])
            V.reciprocal(nr[1][:], nr[1][:])
            dve.drain()
            for n in range(8):
                c = n % 4
                gain = vec[:, (V_GL, V_GA)[n // 4] + c:(V_GL, V_GA)[n // 4] + c + 1]
                if n < 4:
                    stt(nt[:], gel[:, c, :], gain, nr[0][:], ALU.mult, ALU.mult).then_inc(s_gt, 1)
                else:
                    stt(nt[:, 0:T].rearrange("p (t n) -> p t n", t=NTT), attT[:, 0:NTT, c, :], gain,
                        nr[1][:, 0:T].rearrange("p (t n) -> p t n", t=NTT), ALU.mult, ALU.mult)
                    dve.drain()
                    stt(nt[:, T:NTOK], attT[:, NTT, c, 0:NB], gain, nr[1][:, T:NTOK],
                        ALU.mult, ALU.mult).then_inc(s_gt, 1)
                dve.wait_ge(s_gH, n + 1)
                V.tensor_tensor(mixL[:, n, :], nt[:], mixH[:, n, :].bitcast(F32), ALU.subtract).then_inc(s_gL, 1)
                dve.drain()
            gains(V_LN2, 32)
            dve.wait_ge(s_xback, 16)
            for n in range(KD):
                dve.wait_ge(s_un, U_OUT + n + 1)
                b0 = 3 * (n % 2)
                g1 = mod[:, 16 + n, 0:1]
                x3 = cols(xT[:, n, :])
                stt(x3[:, 0:2, :], ps[:, b0:b0 + 2, 0:CW], g1, x3[:, 0:2, :], ALU.mult, ALU.add)
                stt(x3[:, 2, 0:TAIL], ps[:, b0 + 2, 0:TAIL], g1, x3[:, 2, 0:TAIL], ALU.mult, ALU.add)
                V.tensor_copy(samp[:, n, :], ps[:, b0 + 2, TAIL:CW])
                dve.drain().then_inc(s_res, 1)

            def sample_residual(gate_at, src):
                V.tensor_tensor(src[:], src[:], mod[:, gate_at:gate_at + KD, 1:], ALU.mult)
                dve.drain()
                V.tensor_tensor(xT[:, :, T:NTOK], xT[:, :, T:NTOK], src[:], ALU.add)
                dve.drain()

            sample_residual(16, samp)
            dve.drain().then_inc(s_res, 1)
            dve.wait_ge(s_su2, KD)
            variance(nr[0][:], 0, D)
            dve.drain()
            V.memset(samp2[:], 0.0).then_inc(s_v2, 1)
            dve.wait_ge(s_r2, 1)
            modulated(nr[0], nt, h2H, h2L, 24, s_t2, s_h2, s_l2)
            dve.drain()

            dve.drain().then_inc(s_af, 1)
            dve.drain().then_inc(s_dne, 1)

            def product(f, b, i=None):
                n2 = i * 4 if i is not None else 0
                n4 = i * 8 if i is not None else 0
                dve.drain()
                dve.wait_ge(s_sg, n2 + (2 * b + f + 2))
                dve.wait_ge(s_un, n4 + (U_FFN + 4 * b + 2 * f + 2))
                V.tensor_tensor(cols(af[:]), wide(3), cols(sg[:]), ALU.mult).then_inc(s_af, 1)

            def product_low(f, par, b, i=None):
                n2 = i * 4 if i is not None else 0
                dve.wait_ge(s_aH, n2 + (2 * b + f + 1))
                V.tensor_tensor(aL[:, 2 * par + f, :], af[:], aH[:, 2 * par + f, :].bitcast(F32),
                                ALU.subtract).then_inc(s_aL, 1)

            def down_add(q, b, i=None):
                n, c = q // NCH, q % NCH
                n24 = i * 48 if i is not None else 0
                w = CW if c < 2 else TAIL
                dve.wait_ge(s_dn, n24 + (24 * b + q + 2))
                xp = xT[:, n, c * CW:c * CW + w]
                if c == 2:
                    V.tensor_tensor(samp2[:, n, :], samp2[:, n, :], ps[:, 6 + q % 2, TAIL:CW], ALU.add)
                stt(xp, ps[:, 6 + q % 2, 0:w], mod[:, 40 + n, 0:1], xp, ALU.mult, ALU.add).then_inc(s_dne, 1)

            for f in range(2):
                product(f, 0)
                product_low(f, 0, 0)
            with dve.Fori(0, FB // 2) as i:
                for t in range(2):
                    b, par = 1 + t, (1 + t) % 2
                    product(0, b, i)
                    product_low(0, par, b, i)
                    product(1, b, i)
                    for q in range(24):
                        if q == 2:
                            product_low(1, par, b, i)
                        down_add(q, b - 1, i)
            dve.drain()
            for q in range(24):
                down_add(q, FB - 1)
            dve.drain()
            sample_residual(40, samp2)
            dve.drain().then_inc(s_y, 1)

        @block.tensor
        def _(pe):
            mm, tr = pe.matmul, pe.transpose

            pe.wait_ge(s_const, 16)
            for i in range(NTT):
                pe.wait_ge(s_x[i], 16)
                for hf in range(2):
                    g = 2 * i + hf
                    if g >= 4:
                        pe.wait_ge((s_xta, s_xtv)[g % 2], (g - 4) // 2 + 1)
                    for k in range(4):
                        ins = tr(ps[:, g % 4, k * P:(k + 1) * P], xin[:, i, (4 * hf + k) * P:(4 * hf + k + 1) * P],
                                 ident)
                    ins.then_inc(s_tr, 1)
            pe.wait_ge(s_small, 16 * 18)
            for k in range(KD):
                ins = tr(ps[:, 4, k * 8:k * 8 + 8], xs_in[:, k * P:(k + 1) * P], ident[0:NB, 0:NB])
            ins.then_inc(s_mt, 1)
            pe.wait_ge(s_csi, 1)
            for k in range(KD):
                ins = tr(ps[:, 7, k * 9:9 + k * 9], c_si[:, k * P:(k + 1) * P], ident[0:9, 0:9])
            ins.then_inc(s_mt, 1)
            tr(ps[:, 5, 0:V_ALL], vrows[:], ident[0:V_ALL, 0:V_ALL])
            tr(ps[:, 5, 128:256], strows[:], ident)
            mm(ps[:, 5, 256:384], ones[0:1, :], grow[0:1, :], start=True, stop=True).then_inc(s_mt, 1)
            pe.wait_ge(s_mte, 2)
            for j in range(12):
                pe.wait_ge(s_ada[j % 4], 16 * (j // 4 + 1))
                for q in range(4):
                    g = 4 * j + q
                    for k in range(KD):
                        ins = mm(ps[:, 6, g * 9:g * 9 + 9], ada[j % 4][:, k, q * P:(q + 1) * P], cT[:, k, :],
                                 start=(k == 0), stop=(k == KD - 1))
                ins.then_inc(s_modk, 1)

            def stats(src, ready, used, b0, n, first=0, per=1):
                for d in range(n):
                    pe.wait_ge(ready, per * (first + d + 1))
                    for c in range(NCH):
                        ins = mm(ps[:, b0 + c, 0:CW], ones, src[(first + d) % 2][:, c * CW:(c + 1) * CW],
                                 start=(d == 0), stop=(d == n - 1))
                    ins.then_inc(used, 1)

            stats(sq, s_sq, s_squ, 0, KD)
            pe.wait_ge(s_l, KD + 1)
            for n in range(27):
                j, i = n // 9, n % 9
                m = P if i < NTT else NB
                w = CHUNKS[j][1]
                if i == 0:
                    pe.wait_ge(s_cL, j + 1)
                if n >= 6:
                    q = n - 6
                    if q % 2:
                        pe.wait_ge(s_pjv, q // 2 + 1)
                    else:
                        pe.wait_ge(s_pja, q // 2 + 1 + (q // 2 - 8 if q >= 18 else 0))
                t0 = i * P
                for k in range(KD):
                    hi, lo = hH[:, k, t0:t0 + m], hL[:, k, t0:t0 + m]
                    wh, wl = cH[j % 2][:, k, 0:w], cL[j % 2][:, k, 0:w]
                    dst = ps[0:m, n % 6, 0:w]
                    mm(dst, hi, wh, start=(k == 0), stop=False)
                    mm(dst, hi, wl, start=False, stop=False)
                    ins = mm(dst, lo, wh, start=False, stop=(k == KD - 1))
                ins.then_inc(s_pj, 1)
            pe.wait_ge(s_pja, 19)
            pe.wait_ge(s_pjv, 13)

            def index_scores(i):
                for h in range(IH):
                    g = IH * (i - FIRST_SEL) + h
                    if h == 0:
                        pe.wait_ge(s_ite, i + 1)
                        pe.wait_ge(s_ikte, i + 1)
                    if g >= 2:
                        pe.wait_ge(s_re, g - 1)
                    for n0, n in halves(P * (i + 1)):
                        dst = ps[:, 2 * (g % 2) + n0 // 512, 0:n]
                        mm(dst, iqT[i % 2][:, h, :], ikT[:, 0, n0:n0 + n], start=True, stop=False)
                        ins = mm(dst, iqT[i % 2][:, h, :], ikT[:, 1, n0:n0 + n], start=False, stop=True)
                    ins.then_inc(s_sc, 1)

            for i in range(NTT):
                s = i % 2
                pe.wait_ge(s_il, 2 * (i + 1))
                if i >= 2:
                    pe.wait_ge(s_ite, i - 1)
                    pe.wait_ge(s_ikte, i - 1)
                for h in range(IH):
                    tr(ps[:, 4 + s, h * P:(h + 1) * P], istk[s][:, h].rearrange("p r d -> p (r d)"), ident)
                for r in range(2):
                    ins = tr(ps[:, 6 + s, r * P:(r + 1) * P], ikstk[s][:, r].rearrange("p c d -> p (c d)"), ident)
                ins.then_inc(s_it, 1)
                if i >= FIRST_SEL:
                    index_scores(i)
            pe.wait_ge(s_ikte, NTT)
            for h in range(IH):
                tr(ps[0:HD, 7, h * 8:h * 8 + 8], iqk[0:NB, NTT, h * HD:(h + 1) * HD], ident[0:NB, 0:NB])
            tr(ps[0:HD, 7, 32:40], iqk[0:NB, NTT, IH * HD:IH * HD + HD], ident[0:NB, 0:NB])
            mm(ps[0:32, 7, 64:68], consts[0:NB, C_E4:C_E4 + 32], iqk[0:NB, NTT, IH * HD + HD:IQK],
               start=True, stop=True).then_inc(s_diw, 1)
            pe.wait_ge(s_re, IH * (NTT - FIRST_SEL))

            def decode_index(b):
                pe.wait_ge(s_die, 2 * (b + 1))
                if b == 0:
                    pe.wait_ge(s_diw, 2)
                for c, (n0, n) in enumerate(halves(NKEY)):
                    ins = mm(ps[0:32, c, 0:n], iqb[:].rearrange("p b k -> p (b k)")[:, 32 * b:32 * b + 32],
                             ikb[b % 2][:, n0:n0 + n], start=(b == 0), stop=(b == NB - 1))
                return ins

            for b in range(NB):
                pe.wait_ge(s_ipg[b % 2], 16 * PG * (b // 2 + 1))
                if b >= 1:
                    pe.wait_ge(s_die, 2 * b)
                for g in range(PG):
                    ins = tr(ps[0:HD, 4 + g // 4, (g % 4) * P:(g % 4 + 1) * P], ipg[b % 2][:, g, :], ident)
                if b >= 1:
                    ins = decode_index(b - 1)
                ins.then_inc(s_dit, 1)
            decode_index(NB - 1).then_inc(s_dis, 1)
            pe.wait_ge(s_dir, 2)
            for c, (n0, n) in enumerate(halves(NKEY)):
                ins = mm(ps[0:NB, 4 + c, 0:n], iwb[:], reld[:, n0:n0 + n], start=True, stop=True)
            ins.then_inc(s_dsc, 1)
            pe.wait_ge(s_qsq, 1)

            def unit(u, hi, lo, b0):
                s = u % SLOTS
                for k in range(KD):
                    for c in range(NCH):
                        cc = slice(c * CW, (c + 1) * CW)
                        dst = ps[:, b0 + c, 0:CW]
                        mm(dst, wH[s][:, k, :], hi[:, k, cc], start=(k == 0), stop=False)
                        mm(dst, wH[s][:, k, :], lo[:, k, cc], start=False, stop=False)
                        ins = mm(dst, wL[s][:, k, :], hi[:, k, cc], start=False, stop=(k == KD - 1))
                ins.then_inc(s_un, 1)

            pe.wait_ge(s_qkr, 1)
            for u in range(NU_LRU):
                pe.wait_ge(s_wL, u + 1)
                if u >= 2:
                    pe.wait_ge(s_lev, u - 1)
                unit(u, hH, hL, 3 * (u % 2))
            pe.wait_ge(s_lev, NU_LRU)
            pe.wait_ge(s_wbd, 64)
            for c in range(LT):
                pe.wait_ge(s_xc, c + 1)
                if c >= 1:
                    pe.wait_ge(s_gs, 2 * c)
                for gate in range(2):
                    for n in range(NCH):
                        ins = mm(ps[:, 3 * gate + n, 0:CW], wbd[:, gate, c, :], lru_t[0][:, n * CW:(n + 1) * CW],
                                 start=True, stop=True)
                ins.then_inc(s_gp, 1)
            pe.wait_ge(s_lh, LT)
            tr(ps[0:80, 3, 0:P], lasts[:], ident).then_inc(s_lt, 1)
            kst = stk[:].rearrange("p h r d -> p (h r d)").rearrange("p (s k r n) -> p s k r n", s=2, k=NKV, r=2)
            for i in range(NTT):
                pe.wait_ge(s_kst, i + 1)
                if i >= 2:
                    pe.wait_ge(s_kte, i - 1)
                for k in range(NKV):
                    for r in range(2):
                        n = 2 * k + r
                        ins = tr(ps[:, 6 + i % 2, n * P:(n + 1) * P], kst[:, i % 2, k, r, :], ident)
                ins.then_inc(s_kt, 1)
            pe.wait_ge(s_kte, NTT)
            pe.wait_ge(s_lte, 1)

            def q_transposed(n):
                item = q_item(n)
                pe.wait_ge(s_ql, tile_of(n) + 1)
                if item >= 2:
                    pe.wait_ge(s_bte, item - 1)
                for h in range(GRP):
                    ins = tr(ps[:, 4 + item % 2, h * P:(h + 1) * P],
                             stk[:, GRP * (n % 2) + h].rearrange("p r d -> p (r d)"), ident)
                ins.then_inc(s_bt, 1)

            def logits(g):
                n = g // GRP
                if g % GRP == 0:
                    pe.wait_ge(s_bte, q_item(n) + 1)
                if g >= 2:
                    pe.wait_ge(s_lm, g - 1)
                for n0, w in halves(P * (tile_of(n) + 1)):
                    dst = ps[:, 2 * (g % 2) + n0 // 512, 0:w]
                    q = qT[:, g % 8, :]
                    mm(dst, q, kT[:, n % 2, 0, n0:n0 + w], start=True, stop=False)
                    ins = mm(dst, q, kT[:, n % 2, 1, n0:n0 + w], start=False, stop=True)
                ins.then_inc(s_lg, 1)

            def transposed(n, k):
                item = first_item(n) + k
                if k == 0:
                    pe.wait_ge(s_ex, GRP * (n + 1))
                pe.wait_ge(s_bte, item - 1)
                for h in range(GRP):
                    ins = tr(ps[:, 4 + item % 2, h * P:(h + 1) * P],
                             lg[(GRP * n + h) % 8][:, k * P:(k + 1) * P], ident)
                ins.then_inc(s_bt, 1)

            def mixed(n, k):
                if k == 0 and n >= 2:
                    pe.wait_ge(s_hd, n - 1)
                pe.wait_ge(s_bte, first_item(n) + k + 1)
                mm(ps[:, 6 + n % 2, :], v1[:, k, n % 2, :], pT[(key_count(n) + k) % 4][:],
                   start=(k == 0), stop=(k == tile_of(n))).then_inc(s_pv, 1)

            pe.wait_ge(s_v1, 1)
            q_transposed(0)
            for h in range(GRP):
                logits(h)
            for n in range(NG):
                i = tile_of(n)
                if n + 1 < NG:
                    q_transposed(n + 1)
                for step in range(max(GRP, i + 1)):
                    if n + 1 < NG and step < GRP:
                        logits(GRP * (n + 1) + step)
                    if step <= i:
                        transposed(n, step)
                        if step >= 1:
                            mixed(n, step - 1)
                mixed(n, i)

            pe.wait_ge(s_hd, NG)
            for c in range(4):
                tr(ps[:, 7, c * 8:c * 8 + 8], qk[0:NB, NTT, c * P:(c + 1) * P], ident[0:NB, 0:NB])
            tr(ps[:, 7, 32:40], qk[0:NB, NTT, NH * HD:QK], ident[0:NB, 0:NB]).then_inc(s_dqt, 1)
            pe.wait_ge(s_sel, 1)
            for c, (n0, n) in enumerate(halves(NKEY)):
                ins = mm(ps[0:64, c, 0:n], consts[0:NB, C_E8:C_E8 + 64], score[0:NB, S_DEC + n0:S_DEC + n0 + n],
                         start=True, stop=False)
            ins.then_inc(s_dlg, 1)

            def decode_logits(b):
                pe.wait_ge(s_dke, 2 * (b + 1))
                for c, (n0, n) in enumerate(halves(NKEY)):
                    ins = mm(ps[0:64, c, 0:n], qb[:].rearrange("p b k -> p (b k)")[:, 64 * b:64 * b + 64],
                             kbT[b % 2][:, n0:n0 + n], start=False, stop=(b == NB - 1))
                ins.then_inc(s_dlg, 1)

            pe.wait_ge(s_dqe, 1)
            for b in range(NB):
                pe.wait_ge(s_kpg[b], 16 * PG)
                if b >= 1:
                    pe.wait_ge(s_dke, 2 * b)
                for g in range(PG):
                    ins = tr(ps[:, 4 + g // 4, (g % 4) * P:(g % 4 + 1) * P], kpg[b][:, g, :], ident)
                ins.then_inc(s_dkt, 1)
                if b >= 1:
                    decode_logits(b - 1)
            decode_logits(NB - 1)
            pe.wait_ge(s_dpn, 1)
            for g in range(PG):
                tr(ps[:, 3, g * 64:(g + 1) * 64], dlg[:, g * P:(g + 1) * P], ident[0:64, 0:64])
            mm(ps[0:NB, 4, 0:64], consts[0:64, C_E8T:C_E8T + NB], ddg[:], start=True, stop=True).then_inc(s_dpt, 1)
            pe.wait_ge(s_dpe, 1)
            mm(ps[:, 5, 0:64], vt[0:NB, NTT, :], ptl[:], start=True, stop=False, skip_group_check=True)
            for b in range(NB):
                pe.wait_ge(s_vpg[b], 16 * PG)
                for g in range(PG):
                    ins = mm(ps[:, 5, 8 * b:8 * b + 8], vpg[b][:, g, :], dpT[:, g, 8 * b:8 * b + 8],
                             start=False, stop=(g == PG - 1), skip_group_check=True)
                ins.then_inc(s_dpu, 1)

            stats(nsq, s_gsq, s_gsu, 0, 4, first=0, per=2)
            stats(nsq, s_gsq, s_gsu, 3, 4, first=4, per=2)
            pe.wait_ge(s_gL, 8)
            for n in range(NU_OUT):
                u = U_OUT + n
                pe.wait_ge(s_wL, u + 1)
                if n >= 2:
                    pe.wait_ge(s_res, n - 1)
                unit(u, mixH, mixL, 3 * (n % 2))
            stats(nsq, s_sq2, s_su2, 0, KD)
            pe.wait_ge(s_l2, KD + 1)

            pe.sem_inc(s_dn, 1)

            def gate_up(u, b, i=None):
                n12 = i * (2 * UPB) if i is not None else 0
                n2 = i * 4 if i is not None else 0
                for k in range(4):
                    pe.wait_ge(s_wL, n12 + (u + k + 1))
                    pe.wait_ge((s_sg, s_af)[k % 2], n2 + (2 * b + k // 2 + 1))
                    unit(u + k, h2H, h2L, 3 * (k % 2))

            def down(u, par, b, i=None):
                n12 = i * (2 * UPB) if i is not None else 0
                n2 = i * 4 if i is not None else 0
                n24 = i * 48 if i is not None else 0
                pe.wait_ge(s_wL, n12 + (u + 2))
                pe.wait_ge(s_aL, n2 + (2 * b + 2))
                for n in range(KD):
                    for c in range(NCH):
                        q = n * NCH + c
                        pe.wait_ge(s_dne, n24 + (24 * b + max(q - 1, 0) + 1))
                        dst = ps[:, 6 + q % 2, 0:CW]
                        cc = slice(c * CW, (c + 1) * CW)
                        for f in range(2):
                            s = (u + f) % SLOTS
                            mm(dst, wH[s][:, n, :], aH[:, 2 * par + f, cc], start=(f == 0), stop=False)
                            mm(dst, wH[s][:, n, :], aL[:, 2 * par + f, cc], start=False, stop=False)
                            ins = mm(dst, wL[s][:, n, :], aH[:, 2 * par + f, cc], start=False, stop=(f == 1))
                        ins.then_inc(s_dn, 1)

            gate_up(U_FFN, 0)
            with pe.Fori(0, FB // 2) as i:
                for q in range(2):
                    u = U_FFN + 4 + UPB * q
                    gate_up(u, 1 + q, i)
                    down(u + 4, q % 2, q, i)
            down(U_ALL - 2, 0, FB - 1)

            pe.wait_ge(s_y, 1)
            for i in range(ALLT):
                m = P if i < NTT else NB
                for hf in range(2):
                    if i >= 2:
                        pe.wait_ge(s_yea, 2 * (i - 2) + hf + 1)
                    for k in range(4):
                        ins = tr(ps[0:m, 2 * (i % 2) + hf, k * P:(k + 1) * P], xT[:, 4 * hf + k, i * P:i * P + m],
                                 ident)
                    ins.then_inc(s_yt, 1)


_INS = ['x_prompt', 'x_sample', 'cache_k', 'cache_v', 'cache_ik', 'state_h', 'state_conv', 'page_table',
        'c_prompt', 'c_sample', 'ada_w', 'ada_b', 'ln1_g', 'w_in', 'conv_w', 'conv_b', 'lru_wa', 'lru_ba',
        'lru_wx', 'lru_bx', 'lru_lambda', 'q_norm_g', 'k_norm_g', 'gn_lru_g', 'gn_att_g', 'w_out', 'ln2_g',
        'w_gate', 'w_up', 'w_down']
_OUTS = [('y_prompt', (1, T, D)), ('y_sample', (NB, 1, D)),
         ('k_prompt', (1, 1, T, NKV, HD)), ('v_prompt', (1, 1, T, NKV, HD)), ('ik_prompt', (1, 1, T, HD)),
         ('h_prompt', (1, 1, LRU)), ('conv_prompt', (1, 1, 3, LRU)),
         ('k_sample', (1, NB, 1, NKV, HD)), ('v_sample', (1, NB, 1, NKV, HD)), ('ik_sample', (1, NB, 1, HD)),
         ('h_sample', (1, NB, LRU)), ('conv_sample', (1, NB, 3, LRU))]


def table():
    c = np.zeros((P, C_ALL), np.float32)
    r = np.arange(P)
    c[:, C_ID:C_ID + P] = np.eye(P)
    c[:, C_CAUS:C_CAUS + P] = np.where(r[None, :] <= r[:, None], 0.0, -3.0e38)
    c[:, C_ONE:C_ONE + P] = 1.0
    c[0:8, C_E4:C_E4 + 32] = np.repeat(np.eye(8), 4, axis=1)
    c[0:32, C_E4T:C_E4T + 8] = np.repeat(np.eye(8), 4, axis=0)
    c[0:32, C_M4:C_M4 + 4] = np.tile(np.eye(4), (8, 1))
    c[0:8, C_E8:C_E8 + 64] = np.repeat(np.eye(8), 8, axis=1)
    c[0:64, C_E8T:C_E8T + 8] = np.repeat(np.eye(8), 8, axis=0)
    freq = (np.float32(500000.0) ** (-np.arange(HALF, dtype=np.float32) / np.float32(HALF))).astype(np.float32)
    pos = np.full((ALLT, P), T, np.float32)
    pos[:NTT] = np.arange(T).reshape(NTT, P)
    ang = (pos[:, :, None] * freq).astype(np.float32).astype(np.float64)
    rope = np.concatenate([np.cos(ang), np.sin(ang)], axis=-1)
    c[:, C_ROPE:] = rope.transpose(1, 0, 2).reshape(P, -1)
    return c


def kernel(**inputs):
    import numpy as _np
    import concourse.bacc as _bacc
    from concourse import mybir as _mybir
    from concourse.bass_utils import run_bass_kernel_spmd as _run

    nc = _bacc.Bacc("TRN2", target_bir_lowering=False, num_devices=1)
    arrays, ins, outs = {}, {}, {}
    for name in _INS:
        x = _np.ascontiguousarray(inputs[name])
        arrays["in_" + name] = x
        ins[name] = nc.dram_tensor("in_" + name, x.shape, _mybir.dt.from_np(x.dtype), kind="ExternalInput").ap()
    x = table()
    arrays["in_consts"] = x
    ins["consts"] = nc.dram_tensor("in_consts", x.shape, _mybir.dt.from_np(x.dtype), kind="ExternalInput").ap()
    for name, shape in _OUTS:
        outs[name] = nc.dram_tensor("out_" + name, shape, _mybir.dt.float32, kind="ExternalOutput").ap()
    build(nc, ins, outs)
    r = _run(nc, [arrays], core_ids=[0])
    return tuple(r.results[0]["out_" + name] for name, _ in _OUTS)
```
